# Optimizing a Trainium2 kernel written in Bass

```python
import jax, jax.numpy as jnp
from jax import lax
import numpy as np

D_MODEL = 1024
BATCH = 1
SEQ = 256
DEPTH = 2

ATTN_GROUPS = ((128, 1), (512, 4), (2048, 16))
N_GROUPS = 3
ATTN_HEADS = 8
ATTN_HEAD_DIM = 128
ATTN_WIDTH = ATTN_HEADS * ATTN_HEAD_DIM
RET_HEADS = 4
RET_KEY_DIM = 256
RET_VAL_DIM = 512
RET_QK_WIDTH = RET_HEADS * RET_KEY_DIM
RET_V_WIDTH = RET_HEADS * RET_VAL_DIM
RET_CHUNK = 128
ROPE_BASE = 10000.0
D_FF = 2816
CONV_WIDTH = 3
PLE_DIM = 256
MAX_POS_OFFSET = 4096
IN_SIZES = (N_GROUPS * 3 * ATTN_WIDTH, RET_QK_WIDTH, RET_QK_WIDTH, RET_V_WIDTH, RET_V_WIDTH, D_MODEL, D_MODEL)
N_IN = sum(IN_SIZES)
DN_ALPHA = (2 * DEPTH) ** 0.25
DN_BETA = (8 * DEPTH) ** -0.25
LN_EPS = 1e-5
GN_EPS = 1e-6

kernel_name = 'hybrid_dilated_attn_retention_convffn_deepnorm'

def layer_norm(x, g, b):
    xf = x.astype(jnp.float32)
    mu = xf.mean(-1, keepdims=True)
    var = jnp.square(xf - mu).mean(-1, keepdims=True)
    return ((xf - mu) * lax.rsqrt(var + LN_EPS) * g + b).astype(x.dtype)

def dilated_window_attention(q, k, v, window, dilation):
    b, s, h, dh = q.shape
    span = window // dilation
    blk = span
    sub_len = -(-s // dilation)
    sub_len = -(-sub_len // blk) * blk
    s_pad = sub_len * dilation
    nb = sub_len // blk

    def to_blocks(t):
        t = jnp.pad(t.astype(jnp.float32), ((0, 0), (0, s_pad - s), (0, 0), (0, 0)))
        t = t.reshape(b, sub_len, dilation, h, dh).transpose(0, 2, 3, 1, 4)
        return t.reshape(b, dilation, h, nb, blk, dh)

    def with_prev(t):
        prev = jnp.pad(t, ((0, 0), (0, 0), (0, 0), (1, 0), (0, 0), (0, 0)))[:, :, :, :-1]
        return jnp.concatenate([prev, t], axis=4)

    qb = to_blocks(q)
    kc = with_prev(to_blocks(k))
    vc = with_prev(to_blocks(v))
    scores = jnp.einsum('brhnqd,brhnkd->brhnqk', qb, kc) * (dh ** -0.5)
    q_idx = jnp.arange(blk)[:, None] + blk
    k_idx = jnp.arange(2 * blk)[None, :]
    dist = q_idx - k_idx
    band = (dist >= 0) & (dist <= span)
    valid = (jnp.arange(nb)[:, None, None] * blk + k_idx[None] - blk) >= 0
    mask = band[None] & valid
    scores = jnp.where(mask, scores, -jnp.inf)
    m = scores.max(-1, keepdims=True)
    pr = jnp.exp(scores - m)
    denom = pr.sum(-1, keepdims=True)
    out = jnp.einsum('brhnqk,brhnkd->brhnqd', pr, vc) / denom
    lse = (m + jnp.log(denom))[..., 0]
    out = out.reshape(b, dilation, h, sub_len, dh).transpose(0, 3, 1, 2, 4).reshape(b, s_pad, h, dh)[:, :s]
    lse = lse.reshape(b, dilation, h, sub_len).transpose(0, 3, 1, 2).reshape(b, s_pad, h)[:, :s]
    return out, lse

def rotary(t, positions):
    half = t.shape[-1] // 2
    freq = jnp.power(ROPE_BASE, -jnp.arange(half, dtype=jnp.float32) / half)
    ang = positions.astype(jnp.float32)[:, :, None, None] * freq
    cos, sin = jnp.cos(ang), jnp.sin(ang)
    t1, t2 = t[..., :half], t[..., half:]
    return jnp.concatenate([t1 * cos - t2 * sin, t1 * sin + t2 * cos], axis=-1)

def chunkwise_retention(q, k, v, positions):
    b, s, h, dk = q.shape
    dv = v.shape[-1]
    c = RET_CHUNK
    nc = s // c
    q = rotary(q.astype(jnp.float32), positions)
    k = rotary(k.astype(jnp.float32), positions) * (dk ** -0.5)
    v = v.astype(jnp.float32)
    log_gamma = jnp.log1p(-jnp.exp2(-5.0 - jnp.arange(h, dtype=jnp.float32)))
    idx = jnp.arange(c, dtype=jnp.float32)
    rel = idx[:, None] - idx[None, :]
    intra_decay = jnp.where(rel >= 0, jnp.exp(log_gamma[:, None, None] * jnp.maximum(rel, 0.0)), 0.0)
    query_decay = jnp.exp(log_gamma[:, None] * (idx + 1.0))[:, :, None]
    key_decay = jnp.exp(log_gamma[:, None] * (c - 1.0 - idx))[:, :, None]
    chunk_decay = jnp.exp(log_gamma * c)[:, None, None]

    def chunks(t):
        return t.reshape(b, nc, c, h, t.shape[-1]).transpose(1, 0, 3, 2, 4)

    def step(state, qkv):
        qc, kc, vc = qkv
        inner = jnp.einsum('bhqk,bhkv->bhqv', jnp.einsum('bhqd,bhkd->bhqk', qc, kc) * intra_decay, vc)
        cross = jnp.einsum('bhqd,bhdv->bhqv', qc, state) * query_decay
        state = chunk_decay * state + jnp.einsum('bhkd,bhkv->bhdv', kc, vc * key_decay)
        return state, inner + cross

    state0 = jnp.zeros((b, h, dk, dv), jnp.float32)
    _, out = lax.scan(step, state0, (chunks(q), chunks(k), chunks(v)))
    return out.transpose(1, 0, 3, 2, 4).reshape(b, s, h, dv)

def head_group_norm(y, g, bias):
    b, s, h, dv = y.shape
    mu = y.mean(-1, keepdims=True)
    var = jnp.square(y - mu).mean(-1, keepdims=True)
    y = (y - mu) * lax.rsqrt(var + GN_EPS)
    return y.reshape(b, s, h * dv) * g + bias

def token_mixer(x, positions, w_in, w_attn_proj, w_ret_proj, ret_gn_g, ret_gn_b, w_out):
    b, s, _ = x.shape
    proj = x @ w_in
    offsets = [int(o) for o in np.cumsum(IN_SIZES)[:-1]]
    attn_qkv, ret_q, ret_k, ret_v, ret_g, gate_a, gate_r = jnp.split(proj, offsets, axis=-1)
    attn_qkv = attn_qkv.reshape(b, s, N_GROUPS, 3, ATTN_HEADS, ATTN_HEAD_DIM)
    outs, lses = [], []
    for gi, (window, dilation) in enumerate(ATTN_GROUPS):
        o, l = dilated_window_attention(attn_qkv[:, :, gi, 0], attn_qkv[:, :, gi, 1], attn_qkv[:, :, gi, 2], window, dilation)
        outs.append(o)
        lses.append(l)
    weights = jax.nn.softmax(jnp.stack(lses, 0), axis=0)[..., None]
    attn = (weights * jnp.stack(outs, 0)).sum(0).reshape(b, s, ATTN_WIDTH).astype(x.dtype)
    ret = chunkwise_retention(ret_q.reshape(b, s, RET_HEADS, RET_KEY_DIM), ret_k.reshape(b, s, RET_HEADS, RET_KEY_DIM), ret_v.reshape(b, s, RET_HEADS, RET_VAL_DIM), positions)
    ret = head_group_norm(ret, ret_gn_g, ret_gn_b)
    ret = (jax.nn.silu(ret_g.astype(jnp.float32)) * ret).astype(x.dtype)
    merged = jax.nn.sigmoid(gate_a) * (attn @ w_attn_proj) + jax.nn.sigmoid(gate_r) * (ret @ w_ret_proj)
    return merged @ w_out

def conv_ffn(x, w_up, conv_w, conv_b, w_down):
    h = x @ w_up
    h = lax.conv_general_dilated(h, conv_w[:, None, :].astype(h.dtype), window_strides=(1,), padding=((CONV_WIDTH - 1, 0),), dimension_numbers=('NWC', 'WIO', 'NWC'), feature_group_count=h.shape[-1]) + conv_b
    gate, up = jnp.split(h, 2, axis=-1)
    return (jax.nn.gelu(gate) * up) @ w_down

def setup_inputs(seed: int = 0) -> dict:
    key = jax.random.key(seed)
    ks = jax.random.split(key, 20)
    f32 = jnp.float32

    def nrm(k, shape, scale):
        return jax.random.normal(k, shape, f32) * scale

    x = nrm(ks[0], (BATCH, SEQ, D_MODEL), 1.0)
    p = nrm(ks[1], (DEPTH, BATCH, SEQ, PLE_DIM), 1.0)
    offset = jax.random.randint(ks[2], (BATCH, 1), 0, MAX_POS_OFFSET, dtype=jnp.int32)
    positions = offset + jnp.arange(SEQ, dtype=jnp.int32)[None, :]
    w_in = nrm(ks[3], (DEPTH, D_MODEL, N_IN), D_MODEL ** -0.5)
    w_attn_proj = nrm(ks[4], (DEPTH, ATTN_WIDTH, D_MODEL), ATTN_WIDTH ** -0.5)
    w_ret_proj = nrm(ks[5], (DEPTH, RET_V_WIDTH, D_MODEL), RET_V_WIDTH ** -0.5)
    ret_gn_g = 1.0 + nrm(ks[6], (DEPTH, RET_V_WIDTH), 0.02)
    ret_gn_b = nrm(ks[7], (DEPTH, RET_V_WIDTH), 0.02)
    w_out = nrm(ks[8], (DEPTH, D_MODEL, D_MODEL), D_MODEL ** -0.5 * DN_BETA)
    ln1_g = 1.0 + nrm(ks[9], (DEPTH, D_MODEL), 0.02)
    ln1_b = nrm(ks[10], (DEPTH, D_MODEL), 0.02)
    w_up = nrm(ks[11], (DEPTH, D_MODEL, 2 * D_FF), D_MODEL ** -0.5)
    conv_w = nrm(ks[12], (DEPTH, CONV_WIDTH, 2 * D_FF), CONV_WIDTH ** -0.5)
    conv_b = nrm(ks[13], (DEPTH, 2 * D_FF), 0.02)
    w_down = nrm(ks[14], (DEPTH, D_FF, D_MODEL), D_FF ** -0.5 * DN_BETA)
    w_ple_gate = nrm(ks[15], (DEPTH, D_MODEL, D_MODEL), D_MODEL ** -0.5)
    w_ple_proj = nrm(ks[16], (DEPTH, PLE_DIM, D_MODEL), PLE_DIM ** -0.5 * DN_BETA)
    ln2_g = 1.0 + nrm(ks[17], (DEPTH, D_MODEL), 0.02)
    ln2_b = nrm(ks[18], (DEPTH, D_MODEL), 0.02)
    return {'x': x, 'p': p, 'positions': positions, 'w_in': w_in, 'w_attn_proj': w_attn_proj, 'w_ret_proj': w_ret_proj, 'ret_gn_g': ret_gn_g, 'ret_gn_b': ret_gn_b, 'w_out': w_out, 'ln1_g': ln1_g, 'ln1_b': ln1_b, 'w_up': w_up, 'conv_w': conv_w, 'conv_b': conv_b, 'w_down': w_down, 'w_ple_gate': w_ple_gate, 'w_ple_proj': w_ple_proj, 'ln2_g': ln2_g, 'ln2_b': ln2_b}

def reference(x, p, positions, w_in, w_attn_proj, w_ret_proj, ret_gn_g, ret_gn_b, w_out, ln1_g, ln1_b, w_up, conv_w, conv_b, w_down, w_ple_gate, w_ple_proj, ln2_g, ln2_b):
    for i in range(DEPTH):
        mix = token_mixer(x, positions, w_in[i], w_attn_proj[i], w_ret_proj[i], ret_gn_g[i], ret_gn_b[i], w_out[i])
        x = layer_norm(DN_ALPHA * x + mix, ln1_g[i], ln1_b[i])
        ple = jax.nn.sigmoid(x @ w_ple_gate[i]) * (p[i] @ w_ple_proj[i])
        x = layer_norm(DN_ALPHA * x + conv_ffn(x, w_up[i], conv_w[i], conv_b[i], w_down[i]) + ple, ln2_g[i], ln2_b[i])
    return x


_drawn_inputs = setup_inputs


def setup_inputs(seed=0):
    import zlib

    import numpy as np

    out = dict(_drawn_inputs(seed))
    spreads = {}
    factors = {'ret_gn_g': 8.0, 'ret_gn_b': 8.0, 'conv_b': 6.12}
    for name, (base, spread) in spreads.items():
        noise = np.random.default_rng([zlib.crc32(name.encode()), seed]).standard_normal(out[name].shape)
        drawn = base * np.exp(spread * noise) if base else spread * noise
        out[name] = __import__('jax').numpy.asarray(drawn.astype(out[name].dtype))
    for name, factor in factors.items():
        out[name] = (out[name] * factor).astype(out[name].dtype)
    return out
```

```python
from contextlib import ExitStack

import concourse.bass as bass
import numpy as np
from concourse import mybir

F32 = mybir.dt.float32
F32R = mybir.dt.float32r
I32 = mybir.dt.int32
ACT = mybir.ActivationFunctionType
ALU = mybir.AluOpType
AX = mybir.AxisListType

P = 128
D = 1024
SEQ = 256
DEPTH = 2
TT = SEQ // P
KT = D // P
HEADS = 8
GROUPS = ((128, 1), (512, 4), (2048, 16))
NG = len(GROUPS)
RH = 4
RV = 512
D_FF = 2816
PLE = 256
ALPHA = (2 * DEPTH) ** 0.25
LN_EPS = 1e-5
GN_EPS = 1e-6
ATT_SCALE = float(P) ** -0.5
RET_SCALE = 256.0 ** -0.5
MASKED = -1e30

CH = 256
CE = KT * CH
RING = 3
RQ0 = NG * 3 * D
RK0, RV0, RG0 = RQ0 + D, RQ0 + 2 * D, RQ0 + 4 * D
GA0, GR0 = RQ0 + 6 * D, RQ0 + 7 * D

NJ = 4
C_MIX = 15
C_MERGE = NJ * C_MIX
C_PLE = C_MERGE + 6 * NJ
NF = D_FF // CH
C_MLP = C_PLE + 6
C_LAYER = C_MLP + 3 * NF
assert C_LAYER % RING == 0 and C_MERGE % RING == 0 and C_PLE % RING == 0 and C_MLP % RING == 0

CE_PLE = 2 * 512 + 2 * SEQ

USES = (20 + 4 + 2 + NF, 20 + 4 + 2 + NF, 20 + 4 + 2, 4 + 4 + 2)
U_MERGE = (20, 20, 20, 4)
U_PLE = (24, 24, 24, 8)
U_MLP = (26, 26, 26, 10)

NB = 2 * D_FF // P
PC_CW, PC_CB = 0, 3 * NB
PC_GG = PC_CB + NB
PC_GB = PC_GG + 16
PC_LN = PC_GB + 16
NPC = PC_LN + 4 * KT

CC_MASK = 0
CC_DEC = CC_MASK + NG * 256
CC_ID = CC_DEC + RH * 256
CC_FREQ = CC_ID + P
NCC = CC_FREQ + 1

TWO_PI = 2.0 * np.pi
C1 = 6.28125
C2 = float(np.float32(np.floor((TWO_PI - C1) * 2.0 ** 21) / 2.0 ** 21))
C3 = float(np.float32(TWO_PI - C1 - C2))
ROUND = 12582912.0
PI_IN = 3.1415925


def program(nc, x, xT, positions, w_in, w_attn_proj, w_ret_proj, w_out, w_up, w_down,
            w_ple_gate, ple_operands, ln_rows, feature_params, constants, out):
    ctx = ExitStack()
    with ctx:
        def sb(name, shape, dt=F32):
            return ctx.enter_context(nc.sbuf_tensor(name, shape, dt))

        def sem(name):
            return ctx.enter_context(nc.semaphore(name))

        raw = sb("raw", [P, RING, CE])
        w_hi = sb("w_hi", [P, RING, CE], F32R)
        w_lo = sb("w_lo", [P, RING, CE], F32R)
        X = sb("X", [P, TT, D])
        xT_hi = sb("xT_hi", [P, KT, SEQ], F32R)
        xT_lo = sb("xT_lo", [P, KT, SEQ], F32R)
        attn_hi = sb("attn_hi", [P, HEADS, SEQ], F32R)
        attn_lo = sb("attn_lo", [P, HEADS, SEQ], F32R)
        ret_hi = sb("ret_hi", [P, 16, SEQ], F32R)
        ret_lo = sb("ret_lo", [P, 16, SEQ], F32R)
        mid_hi = sb("mid_hi", [P, 2, SEQ], F32R)
        mid_lo = sb("mid_lo", [P, 2, SEQ], F32R)
        const = sb("const", [P, NCC])
        feat = sb("feat", [P, NPC])
        cosT = sb("cosT", [P, SEQ])
        sinT = sb("sinT", [P, SEQ])
        stat = sb("stat", [P, 96])
        zero_r = sb("zero_r", [P, 512], F32R)
        scratch = sb("scratch", [P, 13568])

        def view(start, shape):
            n = int(np.prod(shape))
            v = scratch[:, start:start + n]
            if len(shape) == 2:
                v = v.rearrange("p (a b) -> p a b", a=shape[0])
            if len(shape) == 3:
                v = v.rearrange("p (a b c) -> p a b c", a=shape[0], b=shape[1])
            return v

        qk = view(0, (6, 2, SEQ))
        att_v = view(3072, (NG, TT, CH))
        prob = view(4608, (1152,))
        probT = view(5760, (2, NG, 384))
        roped = view(8064, (2, 2, SEQ))
        rope_c = view(9088, (2, SEQ))
        rope_s = view(9600, (2, SEQ))
        rv = view(10112, (TT, RV))
        decayed = view(11136, (384,))
        ret_y = view(11520, (TT, RV))
        ret_t = view(9088, (4, SEQ))
        silu = view(12544, (4, SEQ))
        ln_gb = view(0, (2, D))
        Y = view(2048, (TT, D))
        xT_f = view(4096, (KT, SEQ))
        ple = view(6144, (TT, D))
        sig = view(8192, (2, 512))
        prod_r = view(9216, (512,))
        prod_a = view(9728, (512,))
        mid = view(10240, (2, SEQ))
        hpad = view(10752, (4, 258))
        conv = view(11784, (4, SEQ))
        ple_sig = view(12808, (512,))

        mask = const[:, CC_MASK:CC_DEC].rearrange("p (g k) -> p g k", g=NG)
        decay = const[:, CC_DEC:CC_ID].rearrange("p (h k) -> p h k", h=RH)
        ident = const[:, CC_ID:CC_ID + P]

        st_gn = stat[:, 0:12]
        mv_gn = stat[:, 12:16].rearrange("p (t s) -> p t s", t=TT)
        ve_gn = stat[:, 16:18]
        rs_gn = stat[:, 18:20]
        st_ln = stat[:, 20:44].rearrange("p (t s) -> p t s", t=TT)
        mv_ln = stat[:, 44:48].rearrange("p (t s) -> p t s", t=TT)
        ve_ln = stat[:, 48:50]
        rs_ln = stat[:, 50:52]
        neg_max = stat[:, 52:54]
        row_sum = stat[:, 54:56]
        row_inv = stat[:, 56:58]
        row_max = stat[:, 58:60]
        half_neg = stat[:, 60:62]

        bank = [ctx.enter_context(nc.psum_tensor(f"bank{i}", [P, 512], F32)) for i in range(4)]
        acc = [ctx.enter_context(nc.psum_tensor(f"acc{i}", [P, 512], F32)) for i in range(4)]

        raw_loaded = [sem(f"raw_loaded{s}") for s in range(RING)]
        hi_ready = sem("hi_ready")
        lo_ready = sem("lo_ready")
        chunk_done = sem("chunk_done")
        bank_read = [sem(f"bank_read{i}") for i in range(4)]
        const_in, pos_in, xT_in, x_in, feat_in, rows_in, stored = (sem(n) for n in (
            "const_in", "pos_in", "xT_in", "x_in", "feat_in", "rows_in", "stored"))
        angle_step, rotary_ready = sem("angle_step"), sem("rotary_ready")
        exponent_set, zeros_set, hpad_zeroed = sem("exponent_set"), sem("zeros_set"), sem("hpad_zeroed")
        xT_hi_ready, xT_lo_ready = sem("xT_hi_ready"), sem("xT_lo_ready")
        scores_done, scores_masked, row_max_ready, neg_max_ready = (sem(n) for n in (
            "scores_done", "scores_masked", "row_max_ready", "neg_max_ready"))
        exp_done, inv_ready, prob_ready = sem("exp_done"), sem("inv_ready"), sem("prob_ready")
        probT_done, probT_copied, pv_done = sem("probT_done"), sem("probT_copied"), sem("pv_done")
        attn_hi_ready, attn_lo_ready = sem("attn_hi_ready"), sem("attn_lo_ready")
        rope_products, roped_ready = sem("rope_products"), sem("roped_ready")
        ret_scores_done, decayed_ready, ret_av_done = sem("ret_scores_done"), sem("decayed_ready"), sem("ret_av_done")
        gn_stats, gn_mean_var, gn_var_eps, gn_rstd, ret_y_ready = (sem(n) for n in (
            "gn_stats", "gn_mean_var", "gn_var_eps", "gn_rstd", "ret_y_ready"))
        ret_yT_done, ret_affine, ret_gated = sem("ret_yT_done"), sem("ret_affine"), sem("ret_gated")
        ret_hi_ready, ret_lo_ready = sem("ret_hi_ready"), sem("ret_lo_ready")
        mid_ready, mid_hi_ready, mid_lo_ready = sem("mid_ready"), sem("mid_hi_ready"), sem("mid_lo_ready")
        acc_half_done = sem("acc_half_done")
        ln_sum, ln_stats, ln_mean_var, ln_var_eps, ln_rstd, ln_y = (sem(n) for n in (
            "ln_sum", "ln_stats", "ln_mean_var", "ln_var_eps", "ln_rstd", "ln_y"))
        lnT_done, xT_f_act, xT_f_dve = sem("lnT_done"), sem("xT_f_act"), sem("xT_f_dve")
        x_by_g, x_updated = sem("x_by_g"), sem("x_updated")
        x_scaled, residual_ready = sem("x_scaled"), sem("residual_ready")
        ple_ready = sem("ple_ready")
        h_in, conv_first, conv_ready, gelu_ready = sem("h_in"), sem("conv_first"), sem("conv_ready"), sem("gelu_ready")

        block = ctx.enter_context(nc.Block())

        @block.sync
        def _(sp):
            def load(c0, c, src, width=CE):
                s = c % RING
                dst = raw[:, s, 0:width]
                if len(src.shape) == 3:
                    dst = dst.rearrange("p (k n) -> p k n", k=src.shape[1])
                sp.wait_ge(lo_ready, c0 + c + 1)
                sp.dma_start(dst, src).then_inc(raw_loaded[s], 16)

            def part(w, l, k0, nk, n0, n):
                v = w.rearrange("l (k p) n -> l p k n", p=P)
                return v[bass.ds(l, 1), :, bass.ds(k0, nk), bass.ds(n0, n)].rearrange("l p k n -> (l p) k n")

            sp.dma_start(xT_f, xT.rearrange("(k p) t -> p k t", p=P)).then_inc(xT_in, 16)
            with sp.Fori(0, DEPTH) as l:
                with sp.Fori(0, NJ) as j:
                    c0 = sp.snap(l * C_LAYER + j * C_MIX)
                    for c in range(6):
                        load(c0, c, part(w_in, l, 0, KT, j * CH + (3 * (c // 2) + c % 2) * D, CH))
                    load(c0, 6, part(w_in, l, 0, KT, j * CH + RQ0, CH))
                    load(c0, 7, part(w_in, l, 0, KT, j * CH + RK0, CH))
                    for u in range(2):
                        load(c0, 8 + u, part(w_in, l, 0, KT, j * RV + RV0 + u * CH, CH))
                    for g in range(NG):
                        load(c0, 10 + g, part(w_in, l, 0, KT, j * CH + (3 * g + 2) * D, CH))
                    for u in range(2):
                        load(c0, 13 + u, part(w_in, l, 0, KT, j * RV + RG0 + u * CH, CH))
                c0 = sp.snap(l * C_LAYER + C_MERGE)
                load(c0, 0, part(w_in, l, 0, KT, GA0, CH))
                load(c0, 1, part(w_in, l, 0, KT, GR0, CH))
                load(c0, 2, part(w_ret_proj, l, 0, KT, 0, CH))
                load(c0, 3, part(w_ret_proj, l, KT, KT, 0, CH))
                load(c0, 4, part(w_attn_proj, l, 0, KT, 0, CH))
                with sp.Fori(0, NJ - 1) as j:
                    c0 = sp.snap(l * C_LAYER + C_MERGE + j * 6)
                    load(c0, 5, part(w_in, l, 0, KT, j * CH + GA0 + CH, CH))
                    load(c0, 6, part(w_out, l, j * 2, 2, 0, D))
                    load(c0, 7, part(w_in, l, 0, KT, j * CH + GR0 + CH, CH))
                    load(c0, 8, part(w_ret_proj, l, 0, KT, j * CH + CH, CH))
                    load(c0, 9, part(w_ret_proj, l, KT, KT, j * CH + CH, CH))
                    load(c0, 10, part(w_attn_proj, l, 0, KT, j * CH + CH, CH))
                c0 = sp.snap(l * C_LAYER + C_PLE)
                load(c0, -1, part(w_out, l, 2 * NJ - 2, 2, 0, D))
                for u in range(2):
                    load(c0, u, ple_operands[bass.ds(l, 1), u, :, :].rearrange("l p n -> (l p) n"), CE_PLE)
                for j in range(NJ):
                    load(c0, 2 + j, part(w_ple_gate, l, 0, KT, j * CH, CH))
                c0 = sp.snap(l * C_LAYER + C_MLP)
                load(c0, 0, part(w_up, l, 0, KT, 0, CH))
                load(c0, 1, part(w_up, l, 0, KT, D_FF, CH))
                with sp.Fori(0, NF - 1) as i:
                    c0 = sp.snap(l * C_LAYER + C_MLP + i * 3)
                    load(c0, 2, part(w_up, l, 0, KT, i * CH + CH, CH))
                    load(c0, 3, part(w_up, l, 0, KT, i * CH + D_FF + CH, CH))
                    load(c0, 4, part(w_down, l, i * 2, 2, 0, D))
                c0 = sp.snap(l * C_LAYER + C_MLP + 3 * NF)
                load(c0, -1, part(w_down, l, 2 * NF - 2, 2, 0, D))
            sp.wait_ge(x_updated, 2 * DEPTH * TT + 1)
            sp.dma_start(out.rearrange("(t p) n -> p t n", p=P), X[:, :, :]).then_inc(stored, 16)
            sp.wait_ge(stored, 16)

        @block.scalar
        def _(act):
            def to_hi(c0, r0, c):
                s = c % RING
                act.wait_ge(raw_loaded[s], r0 + 16 * (c // RING + 1))
                act.wait_ge(chunk_done, c0 + c + 1)
                nc.scalar.activation(w_hi[:, s, :], raw[:, s, :], ACT.Copy).then_inc(hi_ready, 1)

            def copy_out(c0, c, b, dst, scale=1.0, func=ACT.Copy):
                src = bank[b][:, :]
                if len(dst.shape) == 3:
                    src = src.rearrange("p (a b) -> p a b", a=dst.shape[1])
                act.wait_ge(chunk_done, c0 + c + 1 + RING)
                nc.scalar.activation(dst, src, func, scale=scale).then_inc(bank_read[b], 1)

            def norm_transposed(n, w):
                g0, b0 = PC_LN + 2 * w * KT, PC_LN + (2 * w + 1) * KT
                for t in range(TT):
                    act.wait_ge(lnT_done, n * TT + t + 1)
                    for k in range(4):
                        ins = nc.scalar.activation(xT_f[:, k, t * P:(t + 1) * P], acc[2 * t][:, k * P:(k + 1) * P],
                                                   ACT.Identity, scale=feat[:, g0 + k:g0 + k + 1],
                                                   bias=feat[:, b0 + k:b0 + k + 1])
                    ins.then_inc(xT_f_act, 1)
                    act.wait_ge(xT_f_act, n * TT + t + 1)
                    act.wait_ge(xT_f_dve, n * TT + t + 1)
                    nc.scalar.activation(xT_hi[:, :, t * P:(t + 1) * P], xT_f[:, :, t * P:(t + 1) * P],
                                         ACT.Copy).then_inc(xT_hi_ready, 1)

            act.dma_start(const[:, :], constants).then_inc(const_in, 16)
            act.dma_start(sinT[:, :].bitcast(I32), positions[0:1, :].partition_broadcast(P) if False else
                          positions.rearrange("a t -> (a t)").partition_broadcast(P)).then_inc(pos_in, 16)
            act.dma_start(X[:, :, :], x.rearrange("(t p) n -> p t n", p=P)).then_inc(x_in, 16)
            act.wait_ge(xT_in, 16)
            for t in range(TT):
                nc.scalar.activation(xT_hi[:, :, t * P:(t + 1) * P], xT_f[:, :, t * P:(t + 1) * P],
                                     ACT.Copy).then_inc(xT_hi_ready, 1)
            act.wait_ge(angle_step, 10)
            nc.scalar.activation(sinT[:, :], sinT[:, :], ACT.Sin).then_inc(rotary_ready, 1)
            nc.scalar.activation(cosT[:, :], cosT[:, :], ACT.Sin).then_inc(rotary_ready, 1)

            with act.Fori(0, DEPTH) as l:
                n2 = act.snap(l * 2)
                act.wait_ge(xT_hi_ready, n2 * TT + TT)
                act.wait_ge(xT_lo_ready, n2 * TT + TT)
                act.dma_start(feat[:, :], feature_params[bass.ds(l, 1), :, :].rearrange("l p n -> (l p) n"))\
                   .then_inc(feat_in, 16)
                c0 = act.snap(l * C_LAYER)
                r0 = act.snap(l * (16 * C_LAYER // RING))
                to_hi(c0, r0, 0)
                to_hi(c0, r0, 1)
                act.wait_ge(x_updated, n2 * TT + 1)
                with act.Fori(0, NJ) as j:
                    it = act.snap(l * NJ + j)
                    it2 = act.snap(it * 2)
                    c0 = act.snap(l * C_LAYER + j * C_MIX)
                    r0 = act.snap(l * (16 * C_LAYER // RING) + j * (16 * C_MIX // RING))

                    def exp(a):
                        act.wait_ge(neg_max_ready, it2 + a + 1)
                        nc.scalar.activation(prob[:, 0:384], prob[:, 0:384], ACT.Exp, bias=neg_max[:, 0:1],
                                             accum_out=row_sum[:, 0:1])
                        nc.scalar.activation(prob[:, 384:1152], prob[:, 384:1152], ACT.Exp, bias=neg_max[:, 1:2],
                                             accum_out=row_sum[:, 1:2]).then_inc(exp_done, 1)

                    def copy_probT(a):
                        act.wait_ge(probT_done, it2 + a + 1)
                        for g in range(NG):
                            ins = nc.scalar.activation(probT[:, a, g, :], acc[g][:, 0:384], ACT.Copy)
                        ins.then_inc(probT_copied, 1)

                    for c in range(C_MIX):
                        to_hi(c0, r0, c + 2)
                        if c < 6:
                            copy_out(c0, c, c % 3, qk[:, c, :, :], scale=ATT_SCALE if c % 2 == 0 else 1.0)
                        if c == 7:
                            exp(0)
                        if c in (8, 9):
                            copy_out(c0, c, c % 3, rv[:, :, (c - 8) * CH:(c - 7) * CH])
                        if c in (10, 11, 12):
                            copy_out(c0, c, c % 3, att_v[:, c - 10, :, :])
                        if c == 10:
                            copy_probT(0)
                        if c == 11:
                            exp(1)
                        if c in (13, 14):
                            copy_out(c0, c, c % 3, silu[:, 2 * (c - 13):2 * (c - 12), :], func=ACT.Silu)
                        if c == 13:
                            copy_probT(1)
                    for a in range(2):
                        act.wait_ge(pv_done, it2 + a + 1)
                        nc.scalar.activation(attn_hi[:, bass.ds(j * 2 + a, 1), :],
                                             acc[a][:, 0:SEQ].rearrange("p (a b) -> p a b", a=1),
                                             ACT.Copy).then_inc(attn_hi_ready, 1)
                    act.wait_ge(ret_yT_done, it + 1)
                    act.wait_ge(feat_in, l * 16 + 16)
                    for k in range(4):
                        ins = nc.scalar.activation(ret_t[:, k, :], acc[2 + k // 2][:, (k % 2) * SEQ:(k % 2 + 1) * SEQ],
                                                   ACT.Identity, scale=feat[:, bass.ds(j * 4 + (PC_GG + k), 1)],
                                                   bias=feat[:, bass.ds(j * 4 + (PC_GB + k), 1)])
                    ins.then_inc(ret_affine, 1)
                    act.wait_ge(ret_gated, it + 1)
                    nc.scalar.activation(ret_hi[:, bass.ds(j * 4, 4), :], ret_t, ACT.Copy).then_inc(ret_hi_ready, 1)

                c0 = act.snap(l * C_LAYER + C_MERGE)
                r0 = act.snap(l * (16 * C_LAYER // RING) + 16 * C_MERGE // RING)
                act.wait_ge(ret_lo_ready, l * NJ + NJ)
                act.dma_start(ln_gb, ln_rows[bass.ds(l, 1), 0:2 * D].rearrange("l n -> (l n)")
                              .partition_broadcast(P).rearrange("p (r n) -> p r n", r=2)).then_inc(rows_in, 16)
                nm = act.snap(l * (NJ + NF))

                def mid_high(n):
                    act.wait_ge(mid_ready, n)
                    nc.scalar.activation(mid_hi[:, :, :], mid, ACT.Copy).then_inc(mid_hi_ready, 1)

                for c in range(5):
                    to_hi(c0, r0, c + 2)
                    if c < 2:
                        copy_out(c0, c, c, sig[:, c, :], func=ACT.Sigmoid)
                mid_high(nm + 1)
                with act.Fori(0, NJ - 1) as j:
                    c0 = act.snap(l * C_LAYER + C_MERGE + j * 6)
                    r0 = act.snap(l * (16 * C_LAYER // RING) + 16 * C_MERGE // RING + j * 32)
                    nm = act.snap(l * (NJ + NF) + j)
                    for c in range(5, 11):
                        to_hi(c0, r0, c + 2)
                        if c == 5:
                            copy_out(c0, 5, 0, sig[:, 0, :], func=ACT.Sigmoid)
                        if c == 7:
                            copy_out(c0, 7, 1, sig[:, 1, :], func=ACT.Sigmoid)
                    mid_high(nm + 2)

                c0 = act.snap(l * C_LAYER + C_PLE)
                r0 = act.snap(l * (16 * C_LAYER // RING) + 16 * C_PLE // RING)
                to_hi(c0, r0, 1)
                for u in range(2):
                    to_hi(c0, r0, 2 + u)
                    act.wait_ge(chunk_done, c0 + u + 1 + RING)
                    for t in range(TT):
                        nc.scalar.activation(ple[:, t, u * 512:(u + 1) * 512], bank[2 * u + t][:, :],
                                             ACT.Copy).then_inc(bank_read[2 * u + t], 1)
                norm_transposed(n2, 0)
                for j in range(NJ):
                    to_hi(c0, r0, 4 + j)
                    if j:
                        act.wait_ge(ple_ready, l * NJ + j)
                    copy_out(c0, 2 + j, j, ple_sig, func=ACT.Sigmoid)
                act.wait_ge(x_updated, n2 * TT + TT + 1)
                act.dma_start(ln_gb, ln_rows[bass.ds(l, 1), 2 * D:4 * D].rearrange("l n -> (l n)")
                              .partition_broadcast(P).rearrange("p (r n) -> p r n", r=2)).then_inc(rows_in, 16)

                def take_h(c0, c, half, nm, i):
                    src = bank[half][:, :].rearrange("p (a b) -> p a b", a=2)
                    act.wait_ge(chunk_done, c0 + c + 1 + RING)
                    act.wait_ge(mid_ready, nm)
                    nc.scalar.activation(hpad[:, 2 * half:2 * half + 2, 2:2 + SEQ], src, ACT.Copy)
                    for b in range(2):
                        blk = half * (NB // 2) + b
                        ins = nc.scalar.activation(conv[:, 2 * half + b, :], src[:, b, :], ACT.Identity,
                                                   scale=feat[:, bass.ds(i * 2 + (PC_CW + 2 * NB + blk), 1)],
                                                   bias=feat[:, bass.ds(i * 2 + (PC_CB + blk), 1)])
                    ins.then_inc(bank_read[half], 1)

                def gelu_and_high(turn, nm):
                    act.wait_ge(conv_ready, 2 * turn + 1)
                    nc.scalar.activation(conv[:, 0:2, :], conv[:, 0:2, :], ACT.Gelu_apprx_tanh).then_inc(gelu_ready, 1)
                    mid_high(nm)

                c0 = act.snap(l * C_LAYER + C_MLP)
                r0 = act.snap(l * (16 * C_LAYER // RING) + 16 * C_MLP // RING)
                nm = act.snap(l * (NJ + NF) + NJ)
                to_hi(c0, r0, 2)
                take_h(c0, 0, 0, nm, 0)
                take_h(c0, 1, 1, nm, 0)
                with act.Fori(0, NF - 1) as i:
                    c0 = act.snap(l * C_LAYER + C_MLP + i * 3)
                    r0 = act.snap(l * (16 * C_LAYER // RING) + 16 * C_MLP // RING + i * 16)
                    turn = act.snap(l * NF + i)
                    nm = act.snap(l * (NJ + NF) + NJ + i)
                    to_hi(c0, r0, 3)
                    to_hi(c0, r0, 4)
                    gelu_and_high(turn, nm + 1)
                    take_h(c0, 2, 0, nm + 1, i + 1)
                    to_hi(c0, r0, 5)
                    take_h(c0, 3, 1, nm + 1, i + 1)
                act.wait_ge(chunk_done, l * C_LAYER + (C_LAYER - 1 + RING))
                gelu_and_high(l * NF + (NF - 1), l * (NJ + NF) + (NJ + NF))
                norm_transposed(n2 + 1, 1)

        @block.vector
        def _(dve):
            def to_lo(c0, c):
                s = c % RING
                dve.wait_ge(hi_ready, c0 + c + 1)
                nc.vector.tensor_tensor(w_lo[:, s, :], raw[:, s, :], w_hi[:, s, :].bitcast(F32),
                                        ALU.subtract).then_inc(lo_ready, 1)

            def mid_low(n):
                dve.wait_ge(mid_hi_ready, n)
                nc.vector.tensor_tensor(mid_lo[:, :, :], mid, mid_hi[:, :, :].bitcast(F32),
                                        ALU.subtract).then_inc(mid_lo_ready, 1)

            def layer_norm(n, w, c_end, fillers):
                for t in range(TT):
                    q = n * TT + t + 1
                    if t == 0:
                        dve.wait_ge(acc_half_done, n + 1)
                        dve.wait_ge(residual_ready, n + 1)
                    else:
                        dve.wait_ge(chunk_done, c_end + RING)
                    for h in range(2):
                        ins = nc.vector.tensor_tensor(Y[:, t, h * 512:(h + 1) * 512], X[:, t, h * 512:(h + 1) * 512],
                                                      acc[2 * t + h][:, :], ALU.add)
                    ins.then_inc(ln_sum, 1)
                    dve.wait_ge(ln_sum, q)
                    for h in range(2):
                        ins = nc.vector.bn_stats(st_ln[:, t, h * 6:(h + 1) * 6], Y[:, t, h * 512:(h + 1) * 512])
                    ins.then_inc(ln_stats, 1)
                    dve.wait_ge(ln_stats, q)
                    nc.vector.memset(stat[:, 74:75], 0.0)
                    nc.vector.bn_aggr(mv_ln[:, t, :], st_ln[:, t, :]).then_inc(ln_mean_var, 1)
                    dve.wait_ge(ln_mean_var, q)
                    nc.vector.tensor_scalar(ve_ln[:, t:t + 1], mv_ln[:, t, 1:2], LN_EPS, None, ALU.add)\
                      .then_inc(ln_var_eps, 1)
                for t in range(TT):
                    dve.wait_ge(ln_rstd, n * TT + t + 1)
                    nc.vector.tensor_scalar(Y[:, t, :], Y[:, t, :], mv_ln[:, t, 0:1], rs_ln[:, t:t + 1],
                                            ALU.subtract, ALU.mult).then_inc(ln_y, 1)
                for c0, c in fillers:
                    to_lo(c0, c)
                g0, b0 = PC_LN + 2 * w * KT, PC_LN + (2 * w + 1) * KT
                for t in range(TT):
                    dve.wait_ge(lnT_done, n * TT + t + 1)
                    for k in range(4, KT):
                        ins = nc.vector.tensor_scalar(xT_f[:, k, t * P:(t + 1) * P],
                                                      acc[2 * t + 1][:, (k - 4) * P:(k - 3) * P],
                                                      feat[:, g0 + k:g0 + k + 1], feat[:, b0 + k:b0 + k + 1],
                                                      ALU.mult, ALU.add)
                    ins.then_inc(xT_f_dve, 1)
                for t in range(TT):
                    dve.wait_ge(xT_hi_ready, n * TT + t + 1 + TT)
                    nc.vector.tensor_tensor(xT_lo[:, :, t * P:(t + 1) * P], xT_f[:, :, t * P:(t + 1) * P],
                                            xT_hi[:, :, t * P:(t + 1) * P].bitcast(F32),
                                            ALU.subtract).then_inc(xT_lo_ready, 1)

            nc.vector.memset(zero_r[:, :].bitcast(F32), 0.0).then_inc(zeros_set, 1)
            nc.vector.memset(stat[:, 64:65], 0.0).then_inc(lo_ready, RING)
            nc.vector.memset(stat[:, 65:66], 0.0).then_inc(chunk_done, RING)
            for b in range(4):
                nc.vector.memset(stat[:, 66 + b:67 + b], 0.0).then_inc(bank_read[b], 1)
            nc.vector.memset(stat[:, 70:71], 0.0).then_inc(attn_lo_ready, 2)
            nc.vector.memset(stat[:, 71:72], 0.0).then_inc(ret_affine, 1)
            nc.vector.memset(stat[:, 72:73], 0.0).then_inc(ret_hi_ready, 1)
            nc.vector.memset(stat[:, 73:74], 0.0).then_inc(x_updated, 1)
            for t in range(TT):
                dve.wait_ge(xT_hi_ready, t + 1)
                nc.vector.tensor_tensor(xT_lo[:, :, t * P:(t + 1) * P], xT_f[:, :, t * P:(t + 1) * P],
                                        xT_hi[:, :, t * P:(t + 1) * P].bitcast(F32),
                                        ALU.subtract).then_inc(xT_lo_ready, 1)

            steps = [0]

            def angle(ins):
                steps[0] += 1
                ins.then_inc(angle_step, 1)
                dve.wait_ge(angle_step, steps[0])

            ang, turns = rope_c[:, 0, :], rope_c[:, 1, :]
            dve.wait_ge(pos_in, 16)
            dve.wait_ge(const_in, 16)
            angle(nc.vector.tensor_copy(cosT[:, :], sinT[:, :].bitcast(I32)))
            angle(nc.vector.tensor_scalar(ang, cosT[:, :], const[:, CC_FREQ:CC_FREQ + 1], None, ALU.mult))
            angle(nc.vector.tensor_scalar(turns, ang, 1.0 / TWO_PI, ROUND, ALU.mult, ALU.add))
            angle(nc.vector.tensor_scalar(turns, turns, ROUND, None, ALU.subtract))
            for part_of_2pi in (C1, C2, C3):
                angle(nc.vector.scalar_tensor_tensor(out=ang, in0=turns, scalar=-part_of_2pi, in1=ang,
                                                     op0=ALU.mult, op1=ALU.add))
            angle(nc.vector.tensor_scalar(sinT[:, :], ang, PI_IN, -PI_IN, ALU.min, ALU.max))
            angle(nc.vector.scalar_tensor_tensor(out=turns, in0=sinT[:, :], scalar=-1.0, in1=sinT[:, :],
                                                 op0=ALU.mult, op1=ALU.max))
            angle(nc.vector.tensor_scalar(cosT[:, :], turns, -1.0, TWO_PI / 4, ALU.mult, ALU.add))

            with dve.Fori(0, DEPTH) as l:
                c0 = dve.snap(l * C_LAYER)
                to_lo(c0, 0)
                to_lo(c0, 1)
                with dve.Fori(0, NJ) as j:
                    it = dve.snap(l * NJ + j)
                    it2 = dve.snap(it * 2)
                    c0 = dve.snap(l * C_LAYER + j * C_MIX)

                    def rotate(i):
                        src = bank[i]
                        dve.wait_ge(chunk_done, c0 + 6 + i + 1 + RING)
                        if i == 0:
                            dve.wait_ge(rotary_ready, 2)
                            dve.wait_ge(ret_hi_ready, it + 1)
                        for h in range(2):
                            nc.vector.tensor_tensor(rope_c[:, h, :], src[:, h * SEQ:(h + 1) * SEQ], cosT[:, :], ALU.mult)
                        nc.vector.tensor_tensor(rope_s[:, 0, :], src[:, 0:SEQ], sinT[:, :], ALU.mult)\
                          .then_inc(rope_products, 1)
                        nc.vector.tensor_tensor(rope_s[:, 1, :], src[:, SEQ:2 * SEQ], sinT[:, :], ALU.mult)\
                          .then_inc(bank_read[i], 1)
                        dve.wait_ge(bank_read[i], l * USES[i] + j * 5 + 2 + 2)
                        nc.vector.tensor_tensor(roped[:, i, 0, :], rope_c[:, 0, :], rope_s[:, 1, :], ALU.subtract)
                        nc.vector.tensor_tensor(roped[:, i, 1, :], rope_s[:, 0, :], rope_c[:, 1, :], ALU.add)\
                          .then_inc(roped_ready, 1)
                        if i == 0:
                            dve.wait_ge(roped_ready, it2 + 1)

                    def mask_and_max(a):
                        dve.wait_ge(scores_done, it2 + a + 1)
                        nc.vector.tensor_tensor(prob[:, 0:384].rearrange("p (g k) -> p g k", g=NG),
                                                acc[0][:, 0:384].rearrange("p (g k) -> p g k", g=NG),
                                                mask[:, :, P:2 * P], ALU.add)
                        nc.vector.tensor_tensor(prob[:, 384:896].rearrange("p (g k) -> p g k", g=2),
                                                acc[1][:, :].rearrange("p (g k) -> p g k", g=2), mask[:, 0:2, :], ALU.add)
                        nc.vector.tensor_tensor(prob[:, 896:1152], acc[2][:, 0:256], mask[:, 2, :], ALU.add)\
                          .then_inc(scores_masked, 1)
                        dve.wait_ge(scores_masked, it2 + a + 1)
                        nc.vector.reduce_max(row_max[:, 0:1], prob[:, 0:384], AX.X)
                        nc.vector.reduce_max(row_max[:, 1:2], prob[:, 384:1152], AX.X).then_inc(row_max_ready, 1)
                        dve.wait_ge(row_max_ready, it2 + a + 1)
                        nc.vector.tensor_scalar(neg_max, row_max, -1.0, None, ALU.mult).then_inc(neg_max_ready, 1)

                    def normalise(a):
                        dve.wait_ge(exp_done, it2 + a + 1)
                        nc.vector.reciprocal(row_inv, row_sum).then_inc(inv_ready, 1)
                        dve.wait_ge(inv_ready, it2 + a + 1)
                        nc.vector.tensor_scalar(prob[:, 0:384], prob[:, 0:384], row_inv[:, 0:1], None, ALU.mult)
                        nc.vector.tensor_scalar(prob[:, 384:1152], prob[:, 384:1152], row_inv[:, 1:2], None, ALU.mult)\
                          .then_inc(prob_ready, 1)

                    for c in range(C_MIX):
                        to_lo(c0, c + 2)
                        if c == 6:
                            rotate(0)
                        if c == 7:
                            mask_and_max(0)
                            rotate(1)
                        if c == 8:
                            normalise(0)
                        if c == 10:
                            dve.wait_ge(ret_scores_done, it + 1)
                            nc.vector.tensor_tensor(decayed[:, 0:256].rearrange("p (a b) -> p a b", a=1),
                                                    acc[3][:, 0:256].rearrange("p (a b) -> p a b", a=1),
                                                    decay[:, bass.ds(j, 1), :], ALU.mult)
                            nc.vector.tensor_tensor(decayed[:, 256:384].rearrange("p (a b) -> p a b", a=1),
                                                    acc[3][:, 256:384].rearrange("p (a b) -> p a b", a=1),
                                                    decay[:, bass.ds(j, 1), 0:P], ALU.mult).then_inc(decayed_ready, 1)
                        if c == 11:
                            mask_and_max(1)
                        if c == 12:
                            normalise(1)
                            dve.wait_ge(ret_av_done, it + 1)
                            for t, av in enumerate((bank[3], acc[3])):
                                ins = nc.vector.bn_stats(st_gn[:, t * 6:(t + 1) * 6], av[:, :])
                            ins.then_inc(gn_stats, 1)
                            dve.wait_ge(gn_stats, it + 1)
                            nc.vector.memset(stat[:, 75:76], 0.0)
                            for t in range(TT):
                                ins = nc.vector.bn_aggr(mv_gn[:, t, :], st_gn[:, t * 6:(t + 1) * 6])
                            ins.then_inc(gn_mean_var, 1)
                            dve.wait_ge(gn_mean_var, it + 1)
                            nc.vector.tensor_scalar(ve_gn, mv_gn[:, :, 1], GN_EPS, None, ALU.add).then_inc(gn_var_eps, 1)
                        if c == 13:
                            dve.wait_ge(gn_rstd, it + 1)
                            nc.vector.tensor_scalar(ret_y[:, 0, :], bank[3][:, :], mv_gn[:, 0, 0:1], rs_gn[:, 0:1],
                                                    ALU.subtract, ALU.mult).then_inc(bank_read[3], 1)
                            nc.vector.tensor_scalar(ret_y[:, 1, :], acc[3][:, :], mv_gn[:, 1, 0:1], rs_gn[:, 1:2],
                                                    ALU.subtract, ALU.mult).then_inc(ret_y_ready, 1)
                    for a in range(2):
                        dve.wait_ge(attn_hi_ready, it2 + a + 1)
                        nc.vector.tensor_tensor(attn_lo[:, bass.ds(j * 2 + a, 1), :],
                                                acc[a][:, 0:SEQ].rearrange("p (a b) -> p a b", a=1),
                                                attn_hi[:, bass.ds(j * 2 + a, 1), :].bitcast(F32),
                                                ALU.subtract).then_inc(attn_lo_ready, 1)
                    dve.wait_ge(ret_affine, it + 2)
                    nc.vector.tensor_tensor(ret_t, ret_t, silu, ALU.mult).then_inc(ret_gated, 1)
                    dve.wait_ge(ret_hi_ready, it + 2)
                    nc.vector.tensor_tensor(ret_lo[:, bass.ds(j * 4, 4), :], ret_t,
                                            ret_hi[:, bass.ds(j * 4, 4), :].bitcast(F32),
                                            ALU.subtract).then_inc(ret_lo_ready, 1)

                def merge(c0, cs, j, nm):
                    dve.wait_ge(bank_read[1], l * USES[1] + j + (U_MERGE[1] + 2))
                    dve.wait_ge(chunk_done, c0 + cs[0] + 1 + RING)
                    nc.vector.tensor_tensor(prod_r, sig[:, 1, :], bank[2][:, :], ALU.mult).then_inc(bank_read[2], 1)
                    dve.wait_ge(chunk_done, c0 + cs[1] + 1 + RING)
                    nc.vector.tensor_tensor(prod_a, sig[:, 0, :], bank[3][:, :], ALU.mult).then_inc(bank_read[3], 1)
                    dve.wait_ge(bank_read[3], l * USES[3] + j + (U_MERGE[3] + 2))
                    nc.vector.tensor_tensor(mid, prod_r.rearrange("p (a b) -> p a b", a=2),
                                            prod_a.rearrange("p (a b) -> p a b", a=2), ALU.add).then_inc(mid_ready, 1)
                    mid_low(nm)

                c0 = dve.snap(l * C_LAYER + C_MERGE)
                for c in range(5):
                    to_lo(c0, c + 2)
                merge(c0, (3, 4), 0, l * (NJ + NF) + 1)
                with dve.Fori(0, NJ - 1) as j:
                    c0 = dve.snap(l * C_LAYER + C_MERGE + j * 6)
                    for c in range(5, 11):
                        to_lo(c0, c + 2)
                    merge(c0, (9, 10), j + 1, l * (NJ + NF) + j + 2)

                c0 = dve.snap(l * C_LAYER + C_PLE)
                n2 = dve.snap(l * 2)
                to_lo(c0, 1)
                layer_norm(n2, 0, c0, [(c0, 2), (c0, 3)])
                nc.vector.memset(hpad[:, :, 0:2], 0.0).then_inc(hpad_zeroed, 1)
                for j in range(NJ):
                    to_lo(c0, 4 + j)
                    dve.wait_ge(bank_read[j], l * USES[j] + (U_PLE[j] + 1 + 2))
                    v = ple[:, :, j * CH:(j + 1) * CH]
                    nc.vector.tensor_tensor(v, v, ple_sig.rearrange("p (t n) -> p t n", t=TT), ALU.mult)\
                      .then_inc(ple_ready, 1)

                def taps(half, turn, i):
                    dve.wait_ge(bank_read[half], turn + (l * (USES[half] - NF) + (U_MLP[half] + 2)))
                    for tap in (1, 0):
                        for b in range(2):
                            blk = half * (NB // 2) + b
                            ins = nc.vector.scalar_tensor_tensor(
                                out=conv[:, 2 * half + b, :], in0=hpad[:, 2 * half + b, tap:tap + SEQ],
                                scalar=feat[:, bass.ds(i * 2 + (PC_CW + tap * NB + blk), 1)],
                                in1=conv[:, 2 * half + b, :], op0=ALU.mult, op1=ALU.add)
                        if tap:
                            ins.then_inc(conv_first, 1)
                            dve.wait_ge(conv_first, 2 * turn + half + 1)
                    ins.then_inc(conv_ready, 1)

                def gated(turn, nm):
                    dve.wait_ge(conv_ready, 2 * turn + 2)
                    dve.wait_ge(gelu_ready, turn + 1)
                    nc.vector.tensor_tensor(mid, conv[:, 0:2, :], conv[:, 2:4, :], ALU.mult).then_inc(mid_ready, 1)
                    mid_low(nm)

                c0 = dve.snap(l * C_LAYER + C_MLP)
                to_lo(c0, 2)
                turn = dve.snap(l * NF)
                dve.wait_ge(hpad_zeroed, l + 1)
                taps(0, turn, 0)
                taps(1, turn, 0)
                with dve.Fori(0, NF - 1) as i:
                    c0 = dve.snap(l * C_LAYER + C_MLP + i * 3)
                    turn = dve.snap(l * NF + i)
                    nm = dve.snap(l * (NJ + NF) + NJ + i)
                    to_lo(c0, 3)
                    to_lo(c0, 4)
                    gated(turn, nm + 1)
                    next_turn = dve.snap(turn + 1)
                    taps(0, next_turn, i + 1)
                    to_lo(c0, 5)
                    taps(1, next_turn, i + 1)
                gated(l * NF + (NF - 1), l * (NJ + NF) + (NJ + NF))
                layer_norm(n2 + 1, 1, l * C_LAYER + C_LAYER, [])

        @block.gpsimd
        def _(pool):
            nc.gpsimd.memset(half_neg, -0.5).then_inc(exponent_set, 1)
            pool.wait_ge(exponent_set, 1)
            pool.wait_ge(x_in, 16)

            def update_x(n, rows):
                for t in range(TT):
                    pool.wait_ge(ln_var_eps, n * TT + t + 1)
                    nc.gpsimd.tensor_tensor(rs_ln[:, t:t + 1], ve_ln[:, t:t + 1], half_neg[:, 0:1], ALU.pow)\
                      .then_inc(ln_rstd, 1)
                pool.wait_ge(rows_in, rows)
                for t in range(TT):
                    pool.wait_ge(ln_y, n * TT + t + 1)
                    nc.gpsimd.tensor_tensor(X[:, t, :], Y[:, t, :], ln_gb[:, 0, :], ALU.mult).then_inc(x_by_g, 1)
                    pool.wait_ge(x_by_g, n * TT + t + 1)
                    nc.gpsimd.tensor_tensor(X[:, t, :], X[:, t, :], ln_gb[:, 1, :], ALU.add).then_inc(x_updated, 1)

            with pool.Fori(0, DEPTH) as l:
                n2 = pool.snap(l * 2)
                pool.wait_ge(x_updated, n2 * TT + 1)
                nc.gpsimd.tensor_tensor(stat[:, 76:77], half_neg[:, 0:1], half_neg[:, 1:2], ALU.add)
                nc.gpsimd.tensor_scalar(X[:, :, :], X[:, :, :], ALPHA, 0.0, ALU.mult, ALU.add).then_inc(residual_ready, 1)
                with pool.Fori(0, NJ) as j:
                    pool.wait_ge(gn_var_eps, l * NJ + j + 1)
                    nc.gpsimd.tensor_tensor(rs_gn, ve_gn, half_neg, ALU.pow).then_inc(gn_rstd, 1)
                update_x(n2, l * 32 + 16)
                pool.wait_ge(x_updated, n2 * TT + TT + 1)
                nc.gpsimd.tensor_tensor(stat[:, 77:78], half_neg[:, 0:1], half_neg[:, 1:2], ALU.add)
                nc.gpsimd.tensor_scalar(X[:, :, :], X[:, :, :], ALPHA, 0.0, ALU.mult, ALU.add).then_inc(x_scaled, 1)
                pool.wait_ge(x_scaled, l + 1)
                pool.wait_ge(ple_ready, l * NJ + NJ)
                nc.gpsimd.tensor_tensor(X[:, :, :], X[:, :, :], ple, ALU.add).then_inc(residual_ready, 1)
                update_x(n2 + 1, l * 32 + 32)

        @block.tensor
        def _(pe):
            mm = nc.tensor.matmul

            def split_product(dst, st_hi, st_lo, mv_hi, mv_lo, start, stop):
                mm(dst, st_hi, mv_hi, start=start, stop=False)
                mm(dst, st_hi, mv_lo, start=False, stop=False)
                return mm(dst, st_lo, mv_hi, start=False, stop=stop)

            def weights_ready(c0, c):
                pe.wait_ge(lo_ready, c0 + c + 1 + RING)

            def transposed(c0, c, b, src_hi, src_lo, k0=0, start=True, stop=True):
                weights_ready(c0, c)
                s = c % RING
                for m in range(2):
                    for k in range(KT):
                        o = k * CH + m * P
                        ins = split_product(bank[b][:, m * SEQ:(m + 1) * SEQ], w_hi[:, s, o:o + P], w_lo[:, s, o:o + P],
                                            src_hi[:, k0 + k, :], src_lo[:, k0 + k, :],
                                            start and k == 0, stop and k == KT - 1 and (start or m == 1))
                ins.then_inc(chunk_done, 1)

            def by_token(c0, c, b):
                weights_ready(c0, c)
                s = c % RING
                for t in range(TT):
                    for k in range(KT):
                        ins = split_product(bank[b][:, t * CH:(t + 1) * CH],
                                            xT_hi[:, k, t * P:(t + 1) * P], xT_lo[:, k, t * P:(t + 1) * P],
                                            w_hi[:, s, k * CH:(k + 1) * CH], w_lo[:, s, k * CH:(k + 1) * CH],
                                            k == 0, k == KT - 1)
                ins.then_inc(chunk_done, 1)

            def clear(dst):
                mm(dst, zero_r[:, 0:P], zero_r[:, :], start=True, stop=False)

            def from_mid(c0, c, n, last=False):
                pe.wait_ge(mid_lo_ready, n)
                weights_ready(c0, c)
                s = c % RING
                for t in range(TT):
                    for h in range(2):
                        for k in range(2):
                            o = k * D + h * 512
                            ins = split_product(acc[2 * t + h][:, :],
                                                mid_hi[:, k, t * P:(t + 1) * P], mid_lo[:, k, t * P:(t + 1) * P],
                                                w_hi[:, s, o:o + 512], w_lo[:, s, o:o + 512], False, last and k == 1)
                    if last and t == 0:
                        ins.then_inc(acc_half_done, 1)
                ins.then_inc(chunk_done, 1)

            def transpose_y(n):
                for t in range(TT):
                    pe.wait_ge(ln_y, n * TT + t + 1)
                    for k in range(KT):
                        ins = nc.tensor.transpose(acc[2 * t + k // 4][:, (k % 4) * P:(k % 4 + 1) * P],
                                                  Y[:, t, k * P:(k + 1) * P], ident)
                    ins.then_inc(lnT_done, 1)

            pe.wait_ge(const_in, 16)
            pe.wait_ge(zeros_set, 1)
            with pe.Fori(0, DEPTH) as l:
                with pe.Fori(0, NJ) as j:
                    pe.wait_ge(xT_lo_ready, l * (2 * TT) + TT)
                    it = pe.snap(l * NJ + j)
                    it2 = pe.snap(it * 2)
                    c0 = pe.snap(l * C_LAYER + j * C_MIX)
                    used = [pe.snap(l * USES[b] + j * 5) for b in range(3)]

                    def scores(a):
                        for g in range(NG):
                            mm(acc[0][:, g * P:(g + 1) * P], qk[:, 2 * g, a, 0:P], qk[:, 2 * g + 1, a, 0:P],
                               start=True, stop=True)
                        for g in range(NG):
                            ins = mm(acc[1 + g // 2][:, (g % 2) * SEQ:(g % 2 + 1) * SEQ],
                                     qk[:, 2 * g, a, P:SEQ], qk[:, 2 * g + 1, a, :], start=True, stop=True)
                        ins.then_inc(scores_done, 1)

                    def transpose_prob(a):
                        pe.wait_ge(prob_ready, it2 + a + 1)
                        for g in range(NG):
                            for o, src in enumerate((g * P, 384 + g * 256, 384 + g * 256 + P)):
                                ins = nc.tensor.transpose(acc[g][:, o * P:(o + 1) * P], prob[:, src:src + P], ident)
                        ins.then_inc(probT_done, 1)

                    def attend(a):
                        for g in range(NG):
                            mm(acc[a][:, 0:SEQ], att_v[:, g, 0, a * P:(a + 1) * P], probT[:, a, g, 0:SEQ],
                               start=(g == 0), stop=False)
                            ins = mm(acc[a][:, P:SEQ], att_v[:, g, 1, a * P:(a + 1) * P], probT[:, a, g, SEQ:384],
                                     start=False, stop=(g == NG - 1))
                        ins.then_inc(pv_done, 1)

                    for c in range(C_MIX):
                        b = c % 3
                        pe.wait_ge(bank_read[b], used[b] + (c // 3 + 1))
                        if c in (8, 9, 10, 11, 12):
                            by_token(c0, c, b)
                        else:
                            transposed(c0, c, b, xT_hi, xT_lo)
                        if c == 6:
                            pe.wait_ge(bank_read[2], used[2] + 3)
                            pe.wait_ge(attn_lo_ready, it2 + 2)
                            pe.wait_ge(ret_affine, it + 1)
                            scores(0)
                        if c == 9:
                            pe.wait_ge(roped_ready, it2 + 2)
                            for h in range(2):
                                mm(acc[3][:, 0:SEQ], roped[:, 1, h, 0:P], roped[:, 0, h, :], start=(h == 0), stop=(h == 1))
                            for h in range(2):
                                ins = mm(acc[3][:, SEQ:384], roped[:, 1, h, P:SEQ], roped[:, 0, h, P:SEQ],
                                         start=(h == 0), stop=(h == 1))
                            ins.then_inc(ret_scores_done, 1)
                            transpose_prob(0)
                        if c == 10:
                            pe.wait_ge(probT_copied, it2 + 1)
                            scores(1)
                        if c == 11:
                            pe.wait_ge(decayed_ready, it + 1)
                            pe.wait_ge(bank_read[0], used[0] + 5)
                            pe.wait_ge(bank_read[3], l * USES[3] + j + 1)
                            mm(bank[3][:, :], decayed[:, 0:P], rv[:, 0, :], start=True, stop=True)
                            mm(acc[3][:, :], decayed[:, P:SEQ], rv[:, 0, :], start=True, stop=False)
                            mm(acc[3][:, :], decayed[:, SEQ:384], rv[:, 1, :], start=False, stop=True)\
                                .then_inc(ret_av_done, 1)
                        if c == 13:
                            transpose_prob(1)
                    pe.wait_ge(probT_copied, it2 + 2)
                    pe.wait_ge(bank_read[0], used[0] + 6)
                    attend(0)
                    attend(1)
                    pe.wait_ge(ret_y_ready, it + 1)
                    for t in range(TT):
                        for k in range(4):
                            ins = nc.tensor.transpose(acc[2 + k // 2][:, (k % 2) * SEQ + t * P:(k % 2) * SEQ + (t + 1) * P],
                                                      ret_y[:, t, k * P:(k + 1) * P], ident)
                    ins.then_inc(ret_yT_done, 1)

                def gate(c0, c, b, j):
                    pe.wait_ge(bank_read[b], l * USES[b] + j + (U_MERGE[b] + 1))
                    transposed(c0, c, b, xT_hi, xT_lo)

                def mixers(c0, c, j):
                    pe.wait_ge(bank_read[2], l * USES[2] + j + (U_MERGE[2] + 1))
                    clear(bank[2][:, :])
                    transposed(c0, c, 2, ret_hi, ret_lo, 0, start=False, stop=False)
                    transposed(c0, c + 1, 2, ret_hi, ret_lo, KT, start=False)
                    pe.wait_ge(bank_read[3], l * USES[3] + j + (U_MERGE[3] + 1))
                    transposed(c0, c + 2, 3, attn_hi, attn_lo)

                c0 = pe.snap(l * C_LAYER + C_MERGE)
                gate(c0, 0, 0, 0)
                gate(c0, 1, 1, 0)
                pe.wait_ge(ret_lo_ready, l * NJ + NJ)
                pe.wait_ge(attn_lo_ready, l * (2 * NJ) + 2 * NJ + 2)
                pe.wait_ge(ret_affine, l * NJ + NJ + 1)
                for a in range(4):
                    clear(acc[a][:, :])
                mixers(c0, 2, 0)
                with pe.Fori(0, NJ - 1) as j:
                    c0 = pe.snap(l * C_LAYER + C_MERGE + j * 6)
                    gate(c0, 5, 0, j + 1)
                    from_mid(c0, 6, l * (NJ + NF) + j + 1)
                    gate(c0, 7, 1, j + 1)
                    mixers(c0, 8, j + 1)
                c0 = pe.snap(l * C_LAYER + C_PLE)
                from_mid(c0, -1, l * (NJ + NF) + NJ, last=True)

                for u in range(2):
                    weights_ready(c0, u)
                    for t in range(TT):
                        b = 2 * u + t
                        pe.wait_ge(bank_read[b], l * USES[b] + (U_PLE[b] + 1))
                        for k in range(2):
                            o = 1024 + k * SEQ + t * P
                            ins = split_product(bank[b][:, :], w_hi[:, u, o:o + P], w_lo[:, u, o:o + P],
                                                w_hi[:, u, k * 512:(k + 1) * 512], w_lo[:, u, k * 512:(k + 1) * 512],
                                                k == 0, k == 1)
                    ins.then_inc(chunk_done, 1)
                transpose_y(l * 2)
                pe.wait_ge(xT_lo_ready, l * (2 * TT) + 2 * TT)
                for j in range(NJ):
                    pe.wait_ge(bank_read[j], l * USES[j] + (U_PLE[j] + 2))
                    by_token(c0, 2 + j, j)

                def up(c0, c, half, i):
                    pe.wait_ge(bank_read[half], l * USES[half] + i + (U_MLP[half] + 1))
                    transposed(c0, c, half, xT_hi, xT_lo)

                c0 = pe.snap(l * C_LAYER + C_MLP)
                for a in range(4):
                    clear(acc[a][:, :])
                up(c0, 0, 0, 0)
                up(c0, 1, 1, 0)
                with pe.Fori(0, NF - 1) as i:
                    c0 = pe.snap(l * C_LAYER + C_MLP + i * 3)
                    up(c0, 2, 0, i + 1)
                    up(c0, 3, 1, i + 1)
                    from_mid(c0, 4, l * (NJ + NF) + i + (NJ + 1))
                c0 = pe.snap(l * C_LAYER + C_LAYER)
                from_mid(c0, -1, l * (NJ + NF) + (NJ + NF), last=True)
                transpose_y(l * 2 + 1)


def constant_table():
    t = np.zeros((P, NCC), np.float64)
    q = np.arange(P)[:, None]
    k = np.arange(2 * P)[None, :]
    dist = q + P - k
    for g, (window, dilation) in enumerate(GROUPS):
        ok = (dist >= 0) & (dist <= window) & (dist % dilation == 0)
        t[:, CC_MASK + g * 256:CC_MASK + (g + 1) * 256] = np.where(ok, 0.0, MASKED)
    rel = k - q
    for h in range(RH):
        log_gamma = np.log1p(-2.0 ** (-5.0 - h))
        t[:, CC_DEC + h * 256:CC_DEC + (h + 1) * 256] = np.where(
            rel >= 0, np.exp(log_gamma * np.maximum(rel, 0)), 0.0) * RET_SCALE
    t[:, CC_ID:CC_ID + P] = np.eye(P)
    t = t.astype(np.float32)
    t[:, CC_FREQ] = np.power(np.float32(10000.0), -np.arange(P, dtype=np.float32) / np.float32(P))
    return t


def kernel(**inputs):
    import concourse.bacc as _bacc
    from concourse.bass_utils import run_bass_kernel_spmd as _run

    a = {n: np.ascontiguousarray(v) for n, v in inputs.items()}

    def by_feature(v):
        return v.reshape(DEPTH, -1, P).transpose(0, 2, 1)

    feature_params = np.concatenate(
        [by_feature(a["conv_w"][:, i]) for i in range(3)] +
        [by_feature(a[n]) for n in ("conv_b", "ret_gn_g", "ret_gn_b", "ln1_g", "ln1_b", "ln2_g", "ln2_b")], axis=2)
    wp = a["w_ple_proj"].reshape(DEPTH, 2, P, 2, 512).transpose(0, 3, 2, 1, 4).reshape(DEPTH, 2, P, 1024)
    pt = a["p"].reshape(DEPTH, SEQ, 2, P).transpose(0, 3, 2, 1).reshape(DEPTH, 1, P, 2 * SEQ)
    arrays = {
        "x": a["x"].reshape(SEQ, D), "xT": a["x"].reshape(SEQ, D).T, "positions": a["positions"],
        "w_in": a["w_in"], "w_attn_proj": a["w_attn_proj"], "w_ret_proj": a["w_ret_proj"], "w_out": a["w_out"],
        "w_up": a["w_up"], "w_down": a["w_down"], "w_ple_gate": a["w_ple_gate"],
        "ple_operands": np.concatenate([wp, np.repeat(pt, 2, axis=1)], axis=3),
        "ln_rows": np.concatenate([a["ln1_g"], a["ln1_b"], a["ln2_g"], a["ln2_b"]], axis=1),
        "feature_params": feature_params, "constants": constant_table(),
    }
    arrays = {n: np.ascontiguousarray(v) for n, v in arrays.items()}
    nc = _bacc.Bacc("TRN2", target_bir_lowering=False, num_devices=1, dynamic_dma_scratch_size=1024)
    aps = [nc.dram_tensor(n, v.shape, mybir.dt.from_np(v.dtype), kind="ExternalInput").ap() for n, v in arrays.items()]
    out = nc.dram_tensor("out", (SEQ, D), F32, kind="ExternalOutput").ap()
    program(nc, *aps, out)
    r = _run(nc, [arrays], core_ids=[0])
    return r.results[0]["out"].reshape(1, SEQ, D)
```

```python
from contextlib import ExitStack

import concourse.bass as bass
import numpy as np
from concourse import mybir

F32 = mybir.dt.float32
F32R = mybir.dt.float32r
I32 = mybir.dt.int32
ACT = mybir.ActivationFunctionType
ALU = mybir.AluOpType
AX = mybir.AxisListType

P = 128
D = 1024
SEQ = 256
DEPTH = 2
TT = SEQ // P
KT = D // P
HEADS = 8
GROUPS = ((128, 1), (512, 4), (2048, 16))
NG = len(GROUPS)
RH = 4
RV = 512
D_FF = 2816
PLE = 256
ALPHA = (2 * DEPTH) ** 0.25
LN_EPS = 1e-5
GN_EPS = 1e-6
ATT_SCALE = float(P) ** -0.5
RET_SCALE = 256.0 ** -0.5
MASKED = -1e30

CH = 256
CE = KT * CH
RING = 3
RQ0 = NG * 3 * D
RK0, RV0, RG0 = RQ0 + D, RQ0 + 2 * D, RQ0 + 4 * D
GA0, GR0 = RQ0 + 6 * D, RQ0 + 7 * D

NJ = 4
C_MIX = 15
C_MERGE = NJ * C_MIX
C_PLE = C_MERGE + 6 * NJ
NF = D_FF // CH
C_MLP = C_PLE + 6
C_LAYER = C_MLP + 3 * NF
assert C_LAYER % RING == 0 and C_MERGE % RING == 0 and C_PLE % RING == 0 and C_MLP % RING == 0

CE_PLE = 2 * 512 + 2 * SEQ

USES = (20 + 4 + 2 + NF, 20 + 4 + 2 + NF, 20 + 4 + 2, 4 + 4 + 2)
U_MERGE = (20, 20, 20, 4)
U_PLE = (24, 24, 24, 8)
U_MLP = (26, 26, 26, 10)

NB = 2 * D_FF // P
PC_CW, PC_CB = 0, 3 * NB
PC_GG = PC_CB + NB
PC_GB = PC_GG + 16
PC_LN = PC_GB + 16
NPC = PC_LN + 4 * KT

CC_MASK = 0
CC_DEC = CC_MASK + NG * 256
CC_ID = CC_DEC + RH * 256
CC_FREQ = CC_ID + P
NCC = CC_FREQ + 1

TWO_PI = 2.0 * np.pi
C1 = 6.28125
C2 = float(np.float32(np.floor((TWO_PI - C1) * 2.0 ** 21) / 2.0 ** 21))
C3 = float(np.float32(TWO_PI - C1 - C2))
ROUND = 12582912.0
PI_IN = 3.1415925


def program(nc, x, xT, positions, w_in, w_attn_proj, w_ret_proj, w_out, w_up, w_down,
            w_ple_gate, ple_operands, ln_rows, feature_params, constants, out):
    ctx = ExitStack()
    with ctx:
        def sb(name, shape, dt=F32):
            return ctx.enter_context(nc.sbuf_tensor(name, shape, dt))

        def sem(name):
            return ctx.enter_context(nc.semaphore(name))

        raw = sb("raw", [P, RING, CE])
        w_hi = sb("w_hi", [P, RING, CE], F32R)
        w_lo = sb("w_lo", [P, RING, CE], F32R)
        X = sb("X", [P, TT, D])
        xT_hi = sb("xT_hi", [P, KT, SEQ], F32R)
        xT_lo = sb("xT_lo", [P, KT, SEQ], F32R)
        attn_hi = sb("attn_hi", [P, HEADS, SEQ], F32R)
        attn_lo = sb("attn_lo", [P, HEADS, SEQ], F32R)
        ret_hi = sb("ret_hi", [P, 16, SEQ], F32R)
        ret_lo = sb("ret_lo", [P, 16, SEQ], F32R)
        mid_hi = sb("mid_hi", [P, 2, SEQ], F32R)
        mid_lo = sb("mid_lo", [P, 2, SEQ], F32R)
        const = sb("const", [P, NCC])
        feat = sb("feat", [P, NPC])
        cosT = sb("cosT", [P, SEQ])
        sinT = sb("sinT", [P, SEQ])
        stat = sb("stat", [P, 96])
        zero_r = sb("zero_r", [P, 512], F32R)
        scratch = sb("scratch", [P, 13568])

        def view(start, shape):
            n = int(np.prod(shape))
            v = scratch[:, start:start + n]
            if len(shape) == 2:
                v = v.rearrange("p (a b) -> p a b", a=shape[0])
            if len(shape) == 3:
                v = v.rearrange("p (a b c) -> p a b c", a=shape[0], b=shape[1])
            return v

        qk = view(0, (6, 2, SEQ))
        att_v = view(3072, (NG, TT, CH))
        prob = view(4608, (1152,))
        probT = view(5760, (2, NG, 384))
        roped = view(8064, (2, 2, SEQ))
        rope_c = view(9088, (2, SEQ))
        rope_s = view(9600, (2, SEQ))
        rv = view(10112, (TT, RV))
        decayed = view(11136, (384,))
        ret_y = view(11520, (TT, RV))
        ret_t = view(9088, (4, SEQ))
        silu = view(12544, (4, SEQ))
        ln_gb = view(0, (2, D))
        Y = view(2048, (TT, D))
        xT_f = view(4096, (KT, SEQ))
        ple = view(6144, (TT, D))
        sig = view(8192, (2, 512))
        prod_r = view(9216, (512,))
        prod_a = view(9728, (512,))
        mid = view(10240, (2, SEQ))
        hpad = view(10752, (4, 258))
        conv = view(11784, (4, SEQ))
        ple_sig = view(12808, (512,))

        mask = const[:, CC_MASK:CC_DEC].rearrange("p (g k) -> p g k", g=NG)
        decay = const[:, CC_DEC:CC_ID].rearrange("p (h k) -> p h k", h=RH)
        ident = const[:, CC_ID:CC_ID + P]

        st_gn = stat[:, 0:12]
        mv_gn = stat[:, 12:16].rearrange("p (t s) -> p t s", t=TT)
        ve_gn = stat[:, 16:18]
        rs_gn = stat[:, 18:20]
        st_ln = stat[:, 20:44].rearrange("p (t s) -> p t s", t=TT)
        mv_ln = stat[:, 44:48].rearrange("p (t s) -> p t s", t=TT)
        ve_ln = stat[:, 48:50]
        rs_ln = stat[:, 50:52]
        neg_max = stat[:, 52:54]
        row_sum = stat[:, 54:56]
        row_inv = stat[:, 56:58]
        row_max = stat[:, 58:60]
        half_neg = stat[:, 60:62]

        bank = [ctx.enter_context(nc.psum_tensor(f"bank{i}", [P, 512], F32)) for i in range(4)]
        acc = [ctx.enter_context(nc.psum_tensor(f"acc{i}", [P, 512], F32)) for i in range(4)]

        raw_loaded = [sem(f"raw_loaded{s}") for s in range(RING)]
        hi_ready = sem("hi_ready")
        lo_ready = sem("lo_ready")
        chunk_done = sem("chunk_done")
        bank_read = [sem(f"bank_read{i}") for i in range(4)]
        const_in, pos_in, xT_in, x_in, feat_in, rows_in, stored = (sem(n) for n in (
            "const_in", "pos_in", "xT_in", "x_in", "feat_in", "rows_in", "stored"))
        angle_step, rotary_ready = sem("angle_step"), sem("rotary_ready")
        exponent_set, zeros_set, hpad_zeroed = sem("exponent_set"), sem("zeros_set"), sem("hpad_zeroed")
        xT_hi_ready, xT_lo_ready = sem("xT_hi_ready"), sem("xT_lo_ready")
        scores_done, scores_masked, row_max_ready, neg_max_ready = (sem(n) for n in (
            "scores_done", "scores_masked", "row_max_ready", "neg_max_ready"))
        exp_done, inv_ready, prob_ready = sem("exp_done"), sem("inv_ready"), sem("prob_ready")
        probT_done, probT_copied, pv_done = sem("probT_done"), sem("probT_copied"), sem("pv_done")
        attn_hi_ready, attn_lo_ready = sem("attn_hi_ready"), sem("attn_lo_ready")
        rope_products, roped_ready = sem("rope_products"), sem("roped_ready")
        ret_scores_done, decayed_ready, ret_av_done = sem("ret_scores_done"), sem("decayed_ready"), sem("ret_av_done")
        gn_stats, gn_mean_var, gn_var_eps, gn_rstd, ret_y_ready = (sem(n) for n in (
            "gn_stats", "gn_mean_var", "gn_var_eps", "gn_rstd", "ret_y_ready"))
        ret_yT_done, ret_affine, ret_gated = sem("ret_yT_done"), sem("ret_affine"), sem("ret_gated")
        ret_hi_ready, ret_lo_ready = sem("ret_hi_ready"), sem("ret_lo_ready")
        mid_ready, mid_hi_ready, mid_lo_ready = sem("mid_ready"), sem("mid_hi_ready"), sem("mid_lo_ready")
        acc_part_done = sem("acc_part_done")
        ln_sum, ln_stats, ln_mean_var, ln_var_eps, ln_rstd, ln_y = (sem(n) for n in (
            "ln_sum", "ln_stats", "ln_mean_var", "ln_var_eps", "ln_rstd", "ln_y"))
        lnT_done, xT_f_ready = sem("lnT_done"), sem("xT_f_ready")
        x_by_g = [sem(f"x_by_g{t}") for t in range(TT)]
        x_updated = [sem(f"x_updated{t}") for t in range(TT)]
        x_scaled, residual_ready = sem("x_scaled"), sem("residual_ready")
        ple_ready = sem("ple_ready")
        h_in, conv_first, conv_ready, gelu_ready = sem("h_in"), sem("conv_first"), sem("conv_ready"), sem("gelu_ready")

        block = ctx.enter_context(nc.Block())

        @block.sync
        def _(sp):
            def load(c0, c, src, width=CE):
                s = c % RING
                dst = raw[:, s, 0:width]
                if len(src.shape) == 3:
                    dst = dst.rearrange("p (k n) -> p k n", k=src.shape[1])
                sp.wait_ge(lo_ready, c0 + c + 1)
                sp.dma_start(dst, src).then_inc(raw_loaded[s], 16)

            def part(w, l, k0, nk, n0, n):
                v = w.rearrange("l (k p) n -> l p k n", p=P)
                return v[bass.ds(l, 1), :, bass.ds(k0, nk), bass.ds(n0, n)].rearrange("l p k n -> (l p) k n")

            sp.dma_start(xT_f, xT.rearrange("(k p) t -> p k t", p=P)).then_inc(xT_in, 16)
            with sp.Fori(0, DEPTH) as l:
                with sp.Fori(0, NJ) as j:
                    c0 = sp.snap(l * C_LAYER + j * C_MIX)
                    load(c0, 0, part(w_in, l, 0, KT, j * RV + RV0, CH))
                    for c in range(6):
                        load(c0, 1 + c, part(w_in, l, 0, KT, j * CH + (3 * (c // 2) + c % 2) * D, CH))
                    load(c0, 7, part(w_in, l, 0, KT, j * CH + RQ0, CH))
                    load(c0, 8, part(w_in, l, 0, KT, j * CH + RK0, CH))
                    load(c0, 9, part(w_in, l, 0, KT, j * RV + RV0 + CH, CH))
                    for g in range(NG):
                        load(c0, 10 + g, part(w_in, l, 0, KT, j * CH + (3 * g + 2) * D, CH))
                    for u in range(2):
                        load(c0, 13 + u, part(w_in, l, 0, KT, j * RV + RG0 + u * CH, CH))
                c0 = sp.snap(l * C_LAYER + C_MERGE)
                load(c0, 0, part(w_in, l, 0, KT, GA0, CH))
                load(c0, 1, part(w_in, l, 0, KT, GR0, CH))
                load(c0, 2, part(w_ret_proj, l, 0, KT, 0, CH))
                load(c0, 3, part(w_ret_proj, l, KT, KT, 0, CH))
                load(c0, 4, part(w_attn_proj, l, 0, KT, 0, CH))
                with sp.Fori(0, NJ - 1) as j:
                    c0 = sp.snap(l * C_LAYER + C_MERGE + j * 6)
                    load(c0, 5, part(w_in, l, 0, KT, j * CH + GA0 + CH, CH))
                    load(c0, 6, part(w_out, l, j * 2, 2, 0, D))
                    load(c0, 7, part(w_in, l, 0, KT, j * CH + GR0 + CH, CH))
                    load(c0, 8, part(w_ret_proj, l, 0, KT, j * CH + CH, CH))
                    load(c0, 9, part(w_ret_proj, l, KT, KT, j * CH + CH, CH))
                    load(c0, 10, part(w_attn_proj, l, 0, KT, j * CH + CH, CH))
                c0 = sp.snap(l * C_LAYER + C_PLE)
                load(c0, -1, part(w_out, l, 2 * NJ - 2, 2, 0, D))
                for u in range(2):
                    load(c0, u, ple_operands[bass.ds(l, 1), u, :, :].rearrange("l p n -> (l p) n"), CE_PLE)
                for j in range(NJ):
                    load(c0, 2 + j, part(w_ple_gate, l, 0, KT, j * CH, CH))
                c0 = sp.snap(l * C_LAYER + C_MLP)
                load(c0, 0, part(w_up, l, 0, KT, 0, CH))
                load(c0, 1, part(w_up, l, 0, KT, D_FF, CH))
                with sp.Fori(0, NF - 1) as i:
                    c0 = sp.snap(l * C_LAYER + C_MLP + i * 3)
                    load(c0, 2, part(w_up, l, 0, KT, i * CH + CH, CH))
                    load(c0, 3, part(w_up, l, 0, KT, i * CH + D_FF + CH, CH))
                    load(c0, 4, part(w_down, l, i * 2, 2, 0, D))
                c0 = sp.snap(l * C_LAYER + C_MLP + 3 * NF)
                load(c0, -1, part(w_down, l, 2 * NF - 2, 2, 0, D))
            for t in range(TT):
                sp.wait_ge(x_updated[t], 2 * DEPTH + 1)
                sp.dma_start(out[t * P:(t + 1) * P, :], X[:, t, :]).then_inc(stored, 16)
            sp.wait_ge(stored, 16 * TT)

        @block.scalar
        def _(act):
            def to_hi(c0, r0, c):
                s = c % RING
                act.wait_ge(raw_loaded[s], r0 + 16 * (c // RING + 1))
                act.wait_ge(chunk_done, c0 + c + 1)
                nc.scalar.activation(w_hi[:, s, :], raw[:, s, :], ACT.Copy).then_inc(hi_ready, 1)

            def copy_out(c0, c, b, dst, scale=1.0, func=ACT.Copy):
                src = bank[b][:, :]
                if len(dst.shape) == 3:
                    src = src.rearrange("p (a b) -> p a b", a=dst.shape[1])
                act.wait_ge(chunk_done, c0 + c + 1 + RING)
                nc.scalar.activation(dst, src, func, scale=scale).then_inc(bank_read[b], 1)

            def x_high(m):
                for t in range(TT):
                    for h in range(2):
                        act.wait_ge(xT_f_ready, m * 4 + 2 * t + h + 1)
                        v = (slice(None), slice(4 * h, 4 * h + 4), slice(t * P, (t + 1) * P))
                        nc.scalar.activation(xT_hi[v], xT_f[v], ACT.Copy).then_inc(xT_hi_ready, 1)

            act.dma_start(sinT[:, :].bitcast(I32), positions.rearrange("a t -> (a t)").partition_broadcast(P))\
               .then_inc(pos_in, 16)
            for t in range(TT):
                for h in range(2):
                    v = (slice(None), slice(4 * h, 4 * h + 4), slice(t * P, (t + 1) * P))
                    act.wait_ge(xT_in, 16)
                    nc.scalar.activation(xT_hi[v], xT_f[v], ACT.Copy).then_inc(xT_hi_ready, 1)
            to_hi(0, 0, 0)
            act.dma_start(const[:, :], constants).then_inc(const_in, 16)
            to_hi(0, 0, 1)
            act.dma_start(X[:, :, :], x.rearrange("(t p) n -> p t n", p=P)).then_inc(x_in, 16)
            act.wait_ge(angle_step, 10)
            nc.scalar.activation(sinT[:, :], sinT[:, :], ACT.Sin).then_inc(rotary_ready, 1)
            nc.scalar.activation(cosT[:, :], cosT[:, :], ACT.Sin).then_inc(rotary_ready, 1)

            with act.Fori(0, DEPTH) as l:
                n2 = act.snap(l * 2)
                act.wait_ge(xT_lo_ready, n2 * 4 + 4)
                act.dma_start(feat[:, :], feature_params[bass.ds(l, 1), :, :].rearrange("l p n -> (l p) n"))\
                   .then_inc(feat_in, 16)
                for t in range(TT):
                    act.wait_ge(x_updated[t], n2 + 1)
                with act.Fori(0, NJ) as j:
                    it = act.snap(l * NJ + j)
                    it2 = act.snap(it * 2)
                    c0 = act.snap(l * C_LAYER + j * C_MIX)
                    r0 = act.snap(l * (16 * C_LAYER // RING) + j * (16 * C_MIX // RING))

                    def exp(a):
                        act.wait_ge(neg_max_ready, it2 + a + 1)
                        nc.scalar.activation(prob[:, 0:384], prob[:, 0:384], ACT.Exp, bias=neg_max[:, 0:1],
                                             accum_out=row_sum[:, 0:1])
                        nc.scalar.activation(prob[:, 384:1152], prob[:, 384:1152], ACT.Exp, bias=neg_max[:, 1:2],
                                             accum_out=row_sum[:, 1:2]).then_inc(exp_done, 1)

                    def copy_probT(a):
                        act.wait_ge(probT_done, it2 + a + 1)
                        for g in range(NG):
                            ins = nc.scalar.activation(probT[:, a, g, :], acc[g][:, 0:384], ACT.Copy)
                        ins.then_inc(probT_copied, 1)

                    for c in range(C_MIX):
                        to_hi(c0, r0, c + 2)
                        if c in (0, 9):
                            u = c // 9
                            copy_out(c0, c, c % 3, rv[:, :, u * CH:(u + 1) * CH])
                        if c in range(1, 7):
                            copy_out(c0, c, c % 3, qk[:, c - 1, :, :], scale=ATT_SCALE if c % 2 == 1 else 1.0)
                        if c == 8:
                            exp(0)
                        if c == 11:
                            copy_probT(0)
                        if c in (10, 11, 12):
                            copy_out(c0, c, c % 3, att_v[:, c - 10, :, :])
                        if c == 12:
                            exp(1)
                        if c == 14:
                            copy_probT(1)
                        if c in (13, 14):
                            copy_out(c0, c, c % 3, silu[:, 2 * (c - 13):2 * (c - 12), :], func=ACT.Silu)
                    for a in range(2):
                        act.wait_ge(pv_done, it2 + a + 1)
                        nc.scalar.activation(attn_hi[:, bass.ds(j * 2 + a, 1), :],
                                             acc[a][:, 0:SEQ].rearrange("p (a b) -> p a b", a=1),
                                             ACT.Copy).then_inc(attn_hi_ready, 1)
                    act.wait_ge(ret_yT_done, it + 1)
                    act.wait_ge(feat_in, l * 16 + 16)
                    for k in range(4):
                        ins = nc.scalar.activation(ret_t[:, k, :], acc[2 + k // 2][:, (k % 2) * SEQ:(k % 2 + 1) * SEQ],
                                                   ACT.Identity, scale=feat[:, bass.ds(j * 4 + (PC_GG + k), 1)],
                                                   bias=feat[:, bass.ds(j * 4 + (PC_GB + k), 1)])
                    ins.then_inc(ret_affine, 1)
                    act.wait_ge(ret_gated, it + 1)
                    nc.scalar.activation(ret_hi[:, bass.ds(j * 4, 4), :], ret_t, ACT.Copy).then_inc(ret_hi_ready, 1)

                c0 = act.snap(l * C_LAYER + C_MERGE)
                r0 = act.snap(l * (16 * C_LAYER // RING) + 16 * C_MERGE // RING)
                act.wait_ge(ret_lo_ready, l * NJ + NJ)
                act.dma_start(ln_gb, ln_rows[bass.ds(l, 1), 0:2 * D].rearrange("l n -> (l n)")
                              .partition_broadcast(P).rearrange("p (r n) -> p r n", r=2)).then_inc(rows_in, 16)
                nm = act.snap(l * (NJ + NF))

                def mid_high(n):
                    act.wait_ge(mid_ready, n)
                    nc.scalar.activation(mid_hi[:, :, :], mid, ACT.Copy).then_inc(mid_hi_ready, 1)

                for c in range(5):
                    to_hi(c0, r0, c + 2)
                    if c < 2:
                        copy_out(c0, c, c, sig[:, c, :], func=ACT.Sigmoid)
                mid_high(nm + 1)
                with act.Fori(0, NJ - 1) as j:
                    c0 = act.snap(l * C_LAYER + C_MERGE + j * 6)
                    r0 = act.snap(l * (16 * C_LAYER // RING) + 16 * C_MERGE // RING + j * 32)
                    nm = act.snap(l * (NJ + NF) + j)
                    for c in range(5, 11):
                        to_hi(c0, r0, c + 2)
                        if c == 5:
                            copy_out(c0, 5, 0, sig[:, 0, :], func=ACT.Sigmoid)
                        if c == 7:
                            copy_out(c0, 7, 1, sig[:, 1, :], func=ACT.Sigmoid)
                    mid_high(nm + 2)

                c0 = act.snap(l * C_LAYER + C_PLE)
                r0 = act.snap(l * (16 * C_LAYER // RING) + 16 * C_PLE // RING)
                to_hi(c0, r0, 1)
                for u in range(2):
                    to_hi(c0, r0, 2 + u)
                    act.wait_ge(chunk_done, c0 + u + 1 + RING)
                    for t in range(TT):
                        nc.scalar.activation(ple[:, t, u * 512:(u + 1) * 512], bank[2 * u + t][:, :],
                                             ACT.Copy).then_inc(bank_read[2 * u + t], 1)
                x_high(n2)
                for j in range(NJ):
                    to_hi(c0, r0, 4 + j)
                    if j:
                        act.wait_ge(ple_ready, l * NJ + j)
                    copy_out(c0, 2 + j, j, ple_sig, func=ACT.Sigmoid)
                for t in range(TT):
                    act.wait_ge(x_updated[t], n2 + 2)
                act.dma_start(ln_gb, ln_rows[bass.ds(l, 1), 2 * D:4 * D].rearrange("l n -> (l n)")
                              .partition_broadcast(P).rearrange("p (r n) -> p r n", r=2)).then_inc(rows_in, 16)

                def take_h(c0, c, half, nm, i):
                    src = bank[half][:, :].rearrange("p (a b) -> p a b", a=2)
                    act.wait_ge(chunk_done, c0 + c + 1 + RING)
                    act.wait_ge(mid_ready, nm)
                    nc.scalar.activation(hpad[:, 2 * half:2 * half + 2, 2:2 + SEQ], src, ACT.Copy)
                    for b in range(2):
                        blk = half * (NB // 2) + b
                        ins = nc.scalar.activation(conv[:, 2 * half + b, :], src[:, b, :], ACT.Identity,
                                                   scale=feat[:, bass.ds(i * 2 + (PC_CW + 2 * NB + blk), 1)],
                                                   bias=feat[:, bass.ds(i * 2 + (PC_CB + blk), 1)])
                    ins.then_inc(bank_read[half], 1)

                def gelu(turn):
                    act.wait_ge(conv_ready, 2 * turn + 1)
                    nc.scalar.activation(conv[:, 0:2, :], conv[:, 0:2, :], ACT.Gelu_apprx_tanh).then_inc(gelu_ready, 1)

                c0 = act.snap(l * C_LAYER + C_MLP)
                r0 = act.snap(l * (16 * C_LAYER // RING) + 16 * C_MLP // RING)
                nm = act.snap(l * (NJ + NF) + NJ)
                to_hi(c0, r0, 2)
                take_h(c0, 0, 0, nm, 0)
                gelu(act.snap(l * NF))
                take_h(c0, 1, 1, nm, 0)
                with act.Fori(0, NF - 1) as i:
                    c0 = act.snap(l * C_LAYER + C_MLP + i * 3)
                    r0 = act.snap(l * (16 * C_LAYER // RING) + 16 * C_MLP // RING + i * 16)
                    next_turn = act.snap(l * NF + i + 1)
                    nm = act.snap(l * (NJ + NF) + NJ + i)
                    to_hi(c0, r0, 3)
                    to_hi(c0, r0, 4)
                    mid_high(nm + 1)
                    take_h(c0, 2, 0, nm + 1, i + 1)
                    to_hi(c0, r0, 5)
                    gelu(next_turn)
                    take_h(c0, 3, 1, nm + 1, i + 1)
                act.wait_ge(chunk_done, l * C_LAYER + (C_LAYER - 1 + RING))
                mid_high(l * (NJ + NF) + (NJ + NF))
                with act.If(DEPTH - 1 - l):
                    c0 = act.snap(l * C_LAYER + C_LAYER)
                    r0 = act.snap(l * (16 * C_LAYER // RING) + 16 * C_LAYER // RING)
                    to_hi(c0, r0, 0)
                    to_hi(c0, r0, 1)
                    x_high(n2 + 1)

        @block.vector
        def _(dve):
            def to_lo(c0, c):
                s = c % RING
                dve.wait_ge(hi_ready, c0 + c + 1)
                nc.vector.tensor_tensor(w_lo[:, s, :], raw[:, s, :], w_hi[:, s, :].bitcast(F32),
                                        ALU.subtract).then_inc(lo_ready, 1)

            def mid_low(n):
                dve.wait_ge(mid_hi_ready, n)
                nc.vector.tensor_tensor(mid_lo[:, :, :], mid, mid_hi[:, :, :].bitcast(F32),
                                        ALU.subtract).then_inc(mid_lo_ready, 1)

            def normalised(n, c_end):
                dve.wait_ge(residual_ready, n + 1)
                for t in range(TT):
                    for h in range(2):
                        q = 2 * t + h
                        if q < 3:
                            dve.wait_ge(acc_part_done, n * 3 + q + 1)
                        else:
                            dve.wait_ge(chunk_done, c_end + RING)
                        nc.vector.tensor_tensor(Y[:, t, h * 512:(h + 1) * 512], X[:, t, h * 512:(h + 1) * 512],
                                                acc[q][:, :], ALU.add).then_inc(ln_sum, 1)
                        dve.wait_ge(ln_sum, n * 4 + q + 1)
                        ins = nc.vector.bn_stats(st_ln[:, t, h * 6:(h + 1) * 6], Y[:, t, h * 512:(h + 1) * 512])
                    ins.then_inc(ln_stats, 1)
                    dve.wait_ge(ln_stats, n * TT + t + 1)
                    nc.vector.memset(stat[:, 74:75], 0.0)
                    nc.vector.bn_aggr(mv_ln[:, t, :], st_ln[:, t, :]).then_inc(ln_mean_var, 1)
                    dve.wait_ge(ln_mean_var, n * TT + t + 1)
                    nc.vector.tensor_scalar(ve_ln[:, t:t + 1], mv_ln[:, t, 1:2], LN_EPS, None, ALU.add)\
                      .then_inc(ln_var_eps, 1)
                for t in range(TT):
                    dve.wait_ge(ln_rstd, n * TT + t + 1)
                    nc.vector.tensor_scalar(Y[:, t, :], Y[:, t, :], mv_ln[:, t, 0:1], rs_ln[:, t:t + 1],
                                            ALU.subtract, ALU.mult).then_inc(ln_y, 1)

            def x_low(m, t, h):
                dve.wait_ge(xT_hi_ready, m * 4 + 2 * t + h + 1)
                v = (slice(None), slice(4 * h, 4 * h + 4), slice(t * P, (t + 1) * P))
                nc.vector.tensor_tensor(xT_lo[v], xT_f[v], xT_hi[v].bitcast(F32), ALU.subtract)\
                  .then_inc(xT_lo_ready, 1)

            def x_transposed(n, w):
                g0, b0 = PC_LN + 2 * w * KT, PC_LN + (2 * w + 1) * KT
                for t in range(TT):
                    for h in range(2):
                        dve.wait_ge(lnT_done, n * 4 + 2 * t + h + 1)
                        for k in range(4 * h, 4 * h + 4):
                            ins = nc.vector.tensor_scalar(xT_f[:, k, t * P:(t + 1) * P],
                                                          acc[2 * t + h][:, (k % 4) * P:(k % 4 + 1) * P],
                                                          feat[:, g0 + k:g0 + k + 1], feat[:, b0 + k:b0 + k + 1],
                                                          ALU.mult, ALU.add)
                        ins.then_inc(xT_f_ready, 1)
                    for h in range(2):
                        x_low(n + 1, t, h)

            def second_tile(n, rows):
                dve.wait_ge(rows_in, rows)
                dve.wait_ge(ln_y, n * TT + TT)
                nc.vector.tensor_tensor(X[:, 1, :], Y[:, 1, :], ln_gb[:, 0, :], ALU.mult).then_inc(x_by_g[1], 1)
                dve.wait_ge(x_by_g[1], n + 1)
                nc.vector.tensor_tensor(X[:, 1, :], X[:, 1, :], ln_gb[:, 1, :], ALU.add).then_inc(x_updated[1], 1)

            nc.vector.memset(zero_r[:, :].bitcast(F32), 0.0).then_inc(zeros_set, 1)
            nc.vector.memset(stat[:, 64:65], 0.0).then_inc(lo_ready, RING)
            nc.vector.memset(stat[:, 65:66], 0.0).then_inc(chunk_done, RING)
            for b in range(4):
                nc.vector.memset(stat[:, 66 + b:67 + b], 0.0).then_inc(bank_read[b], 1)
            nc.vector.memset(stat[:, 70:71], 0.0).then_inc(attn_lo_ready, 2)
            nc.vector.memset(stat[:, 71:72], 0.0).then_inc(ret_affine, 1)
            nc.vector.memset(stat[:, 72:73], 0.0).then_inc(ret_hi_ready, 1)
            for t in range(TT):
                nc.vector.memset(stat[:, 78 + t:79 + t], 0.0).then_inc(x_updated[t], 1)
            for t in range(TT):
                for h in range(2):
                    x_low(0, t, h)
            to_lo(0, 0)
            to_lo(0, 1)

            steps = [0]

            def angle(ins):
                steps[0] += 1
                ins.then_inc(angle_step, 1)
                dve.wait_ge(angle_step, steps[0])

            ang, turns = rope_c[:, 0, :], rope_c[:, 1, :]
            dve.wait_ge(pos_in, 16)
            dve.wait_ge(const_in, 16)
            angle(nc.vector.tensor_copy(cosT[:, :], sinT[:, :].bitcast(I32)))
            angle(nc.vector.tensor_scalar(ang, cosT[:, :], const[:, CC_FREQ:CC_FREQ + 1], None, ALU.mult))
            angle(nc.vector.tensor_scalar(turns, ang, 1.0 / TWO_PI, ROUND, ALU.mult, ALU.add))
            angle(nc.vector.tensor_scalar(turns, turns, ROUND, None, ALU.subtract))
            for part_of_2pi in (C1, C2, C3):
                angle(nc.vector.scalar_tensor_tensor(out=ang, in0=turns, scalar=-part_of_2pi, in1=ang,
                                                     op0=ALU.mult, op1=ALU.add))
            angle(nc.vector.tensor_scalar(sinT[:, :], ang, PI_IN, -PI_IN, ALU.min, ALU.max))
            angle(nc.vector.scalar_tensor_tensor(out=turns, in0=sinT[:, :], scalar=-1.0, in1=sinT[:, :],
                                                 op0=ALU.mult, op1=ALU.max))
            angle(nc.vector.tensor_scalar(cosT[:, :], turns, -1.0, TWO_PI / 4, ALU.mult, ALU.add))

            with dve.Fori(0, DEPTH) as l:
                with dve.Fori(0, NJ) as j:
                    it = dve.snap(l * NJ + j)
                    it2 = dve.snap(it * 2)
                    c0 = dve.snap(l * C_LAYER + j * C_MIX)

                    def rotate(i):
                        b = i + 1
                        src = bank[b]
                        dve.wait_ge(chunk_done, c0 + 7 + i + 1 + RING)
                        if i == 0:
                            dve.wait_ge(rotary_ready, 2)
                            dve.wait_ge(ret_hi_ready, it + 1)
                        for h in range(2):
                            nc.vector.tensor_tensor(rope_c[:, h, :], src[:, h * SEQ:(h + 1) * SEQ], cosT[:, :], ALU.mult)
                        nc.vector.tensor_tensor(rope_s[:, 0, :], src[:, 0:SEQ], sinT[:, :], ALU.mult)\
                          .then_inc(rope_products, 1)
                        nc.vector.tensor_tensor(rope_s[:, 1, :], src[:, SEQ:2 * SEQ], sinT[:, :], ALU.mult)\
                          .then_inc(bank_read[b], 1)
                        dve.wait_ge(bank_read[b], l * USES[b] + j * 5 + 2 + 2)
                        nc.vector.tensor_tensor(roped[:, i, 0, :], rope_c[:, 0, :], rope_s[:, 1, :], ALU.subtract)
                        nc.vector.tensor_tensor(roped[:, i, 1, :], rope_s[:, 0, :], rope_c[:, 1, :], ALU.add)\
                          .then_inc(roped_ready, 1)
                        if i == 0:
                            dve.wait_ge(roped_ready, it2 + 1)

                    def mask_and_max(a):
                        dve.wait_ge(scores_done, it2 + a + 1)
                        nc.vector.tensor_tensor(prob[:, 0:384].rearrange("p (g k) -> p g k", g=NG),
                                                acc[0][:, 0:384].rearrange("p (g k) -> p g k", g=NG),
                                                mask[:, :, P:2 * P], ALU.add)
                        nc.vector.tensor_tensor(prob[:, 384:896].rearrange("p (g k) -> p g k", g=2),
                                                acc[1][:, :].rearrange("p (g k) -> p g k", g=2), mask[:, 0:2, :], ALU.add)
                        nc.vector.tensor_tensor(prob[:, 896:1152], acc[2][:, 0:256], mask[:, 2, :], ALU.add)\
                          .then_inc(scores_masked, 1)
                        dve.wait_ge(scores_masked, it2 + a + 1)
                        nc.vector.reduce_max(row_max[:, 0:1], prob[:, 0:384], AX.X)
                        nc.vector.reduce_max(row_max[:, 1:2], prob[:, 384:1152], AX.X).then_inc(row_max_ready, 1)
                        dve.wait_ge(row_max_ready, it2 + a + 1)
                        nc.vector.tensor_scalar(neg_max, row_max, -1.0, None, ALU.mult).then_inc(neg_max_ready, 1)

                    def normalise(a):
                        dve.wait_ge(exp_done, it2 + a + 1)
                        nc.vector.reciprocal(row_inv, row_sum).then_inc(inv_ready, 1)
                        dve.wait_ge(inv_ready, it2 + a + 1)
                        nc.vector.tensor_scalar(prob[:, 0:384], prob[:, 0:384], row_inv[:, 0:1], None, ALU.mult)
                        nc.vector.tensor_scalar(prob[:, 384:1152], prob[:, 384:1152], row_inv[:, 1:2], None, ALU.mult)\
                          .then_inc(prob_ready, 1)

                    for c in range(C_MIX):
                        to_lo(c0, c + 2)
                        if c == 7:
                            rotate(0)
                        if c == 8:
                            mask_and_max(0)
                            rotate(1)
                        if c == 9:
                            normalise(0)
                        if c == 11:
                            dve.wait_ge(ret_scores_done, it + 1)
                            nc.vector.tensor_tensor(decayed[:, 0:256].rearrange("p (a b) -> p a b", a=1),
                                                    acc[3][:, 0:256].rearrange("p (a b) -> p a b", a=1),
                                                    decay[:, bass.ds(j, 1), :], ALU.mult)
                            nc.vector.tensor_tensor(decayed[:, 256:384].rearrange("p (a b) -> p a b", a=1),
                                                    acc[3][:, 256:384].rearrange("p (a b) -> p a b", a=1),
                                                    decay[:, bass.ds(j, 1), 0:P], ALU.mult).then_inc(decayed_ready, 1)
                        if c == 12:
                            mask_and_max(1)
                        if c == 13:
                            normalise(1)
                            dve.wait_ge(ret_av_done, it + 1)
                            for t, av in enumerate((bank[3], acc[3])):
                                ins = nc.vector.bn_stats(st_gn[:, t * 6:(t + 1) * 6], av[:, :])
                            ins.then_inc(gn_stats, 1)
                            dve.wait_ge(gn_stats, it + 1)
                            nc.vector.memset(stat[:, 75:76], 0.0)
                            for t in range(TT):
                                ins = nc.vector.bn_aggr(mv_gn[:, t, :], st_gn[:, t * 6:(t + 1) * 6])
                            ins.then_inc(gn_mean_var, 1)
                            dve.wait_ge(gn_mean_var, it + 1)
                            nc.vector.tensor_scalar(ve_gn, mv_gn[:, :, 1], GN_EPS, None, ALU.add).then_inc(gn_var_eps, 1)
                        if c == 14:
                            dve.wait_ge(gn_rstd, it + 1)
                            nc.vector.tensor_scalar(ret_y[:, 0, :], bank[3][:, :], mv_gn[:, 0, 0:1], rs_gn[:, 0:1],
                                                    ALU.subtract, ALU.mult).then_inc(bank_read[3], 1)
                            nc.vector.tensor_scalar(ret_y[:, 1, :], acc[3][:, :], mv_gn[:, 1, 0:1], rs_gn[:, 1:2],
                                                    ALU.subtract, ALU.mult).then_inc(ret_y_ready, 1)
                    for a in range(2):
                        dve.wait_ge(attn_hi_ready, it2 + a + 1)
                        nc.vector.tensor_tensor(attn_lo[:, bass.ds(j * 2 + a, 1), :],
                                                acc[a][:, 0:SEQ].rearrange("p (a b) -> p a b", a=1),
                                                attn_hi[:, bass.ds(j * 2 + a, 1), :].bitcast(F32),
                                                ALU.subtract).then_inc(attn_lo_ready, 1)
                    dve.wait_ge(ret_affine, it + 2)
                    nc.vector.tensor_tensor(ret_t, ret_t, silu, ALU.mult).then_inc(ret_gated, 1)
                    dve.wait_ge(ret_hi_ready, it + 2)
                    nc.vector.tensor_tensor(ret_lo[:, bass.ds(j * 4, 4), :], ret_t,
                                            ret_hi[:, bass.ds(j * 4, 4), :].bitcast(F32),
                                            ALU.subtract).then_inc(ret_lo_ready, 1)

                def merge(c0, cs, j, nm):
                    dve.wait_ge(bank_read[1], l * USES[1] + j + (U_MERGE[1] + 2))
                    dve.wait_ge(chunk_done, c0 + cs[0] + 1 + RING)
                    nc.vector.tensor_tensor(prod_r, sig[:, 1, :], bank[2][:, :], ALU.mult).then_inc(bank_read[2], 1)
                    dve.wait_ge(chunk_done, c0 + cs[1] + 1 + RING)
                    nc.vector.tensor_tensor(prod_a, sig[:, 0, :], bank[3][:, :], ALU.mult).then_inc(bank_read[3], 1)
                    dve.wait_ge(bank_read[3], l * USES[3] + j + (U_MERGE[3] + 2))
                    nc.vector.tensor_tensor(mid, prod_r.rearrange("p (a b) -> p a b", a=2),
                                            prod_a.rearrange("p (a b) -> p a b", a=2), ALU.add).then_inc(mid_ready, 1)
                    mid_low(nm)

                c0 = dve.snap(l * C_LAYER + C_MERGE)
                for c in range(5):
                    to_lo(c0, c + 2)
                merge(c0, (3, 4), 0, l * (NJ + NF) + 1)
                with dve.Fori(0, NJ - 1) as j:
                    c0 = dve.snap(l * C_LAYER + C_MERGE + j * 6)
                    for c in range(5, 11):
                        to_lo(c0, c + 2)
                    merge(c0, (9, 10), j + 1, l * (NJ + NF) + j + 2)

                c0 = dve.snap(l * C_LAYER + C_PLE)
                n2 = dve.snap(l * 2)
                to_lo(c0, 1)
                normalised(n2, c0)
                to_lo(c0, 2)
                to_lo(c0, 3)
                x_transposed(n2, 0)
                second_tile(n2, l * 32 + 16)
                nc.vector.memset(hpad[:, :, 0:2], 0.0).then_inc(hpad_zeroed, 1)
                for j in range(NJ):
                    to_lo(c0, 4 + j)
                    dve.wait_ge(bank_read[j], l * USES[j] + (U_PLE[j] + 1 + 2))
                    v = ple[:, :, j * CH:(j + 1) * CH]
                    nc.vector.tensor_tensor(v, v, ple_sig.rearrange("p (t n) -> p t n", t=TT), ALU.mult)\
                      .then_inc(ple_ready, 1)

                def taps(half, turn, i):
                    dve.wait_ge(bank_read[half], turn + (l * (USES[half] - NF) + (U_MLP[half] + 2)))
                    for tap in (1, 0):
                        for b in range(2):
                            blk = half * (NB // 2) + b
                            ins = nc.vector.scalar_tensor_tensor(
                                out=conv[:, 2 * half + b, :], in0=hpad[:, 2 * half + b, tap:tap + SEQ],
                                scalar=feat[:, bass.ds(i * 2 + (PC_CW + tap * NB + blk), 1)],
                                in1=conv[:, 2 * half + b, :], op0=ALU.mult, op1=ALU.add)
                        if tap:
                            ins.then_inc(conv_first, 1)
                            dve.wait_ge(conv_first, 2 * turn + half + 1)
                    ins.then_inc(conv_ready, 1)

                def gated(turn, nm):
                    dve.wait_ge(conv_ready, 2 * turn + 2)
                    dve.wait_ge(gelu_ready, turn + 1)
                    nc.vector.tensor_tensor(mid, conv[:, 0:2, :], conv[:, 2:4, :], ALU.mult).then_inc(mid_ready, 1)
                    mid_low(nm)

                c0 = dve.snap(l * C_LAYER + C_MLP)
                to_lo(c0, 2)
                turn = dve.snap(l * NF)
                dve.wait_ge(hpad_zeroed, l + 1)
                taps(0, turn, 0)
                taps(1, turn, 0)
                with dve.Fori(0, NF - 1) as i:
                    c0 = dve.snap(l * C_LAYER + C_MLP + i * 3)
                    turn = dve.snap(l * NF + i)
                    nm = dve.snap(l * (NJ + NF) + NJ + i)
                    to_lo(c0, 3)
                    to_lo(c0, 4)
                    gated(turn, nm + 1)
                    next_turn = dve.snap(turn + 1)
                    taps(0, next_turn, i + 1)
                    to_lo(c0, 5)
                    taps(1, next_turn, i + 1)
                gated(l * NF + (NF - 1), l * (NJ + NF) + (NJ + NF))
                c0 = dve.snap(l * C_LAYER + C_LAYER)
                with dve.If(DEPTH - 1 - l):
                    to_lo(c0, 0)
                normalised(n2 + 1, c0)
                with dve.If(DEPTH - 1 - l):
                    to_lo(c0, 1)
                    x_transposed(n2 + 1, 1)
                second_tile(n2 + 1, l * 32 + 32)

        @block.gpsimd
        def _(pool):
            nc.gpsimd.memset(half_neg, -0.5).then_inc(exponent_set, 1)
            pool.wait_ge(exponent_set, 1)
            pool.wait_ge(x_in, 16)

            def update_x(n, rows):
                for t in range(TT):
                    pool.wait_ge(ln_var_eps, n * TT + t + 1)
                    nc.gpsimd.tensor_tensor(rs_ln[:, t:t + 1], ve_ln[:, t:t + 1], half_neg[:, 0:1], ALU.pow)\
                      .then_inc(ln_rstd, 1)
                pool.wait_ge(rows_in, rows)
                pool.wait_ge(ln_y, n * TT + 1)
                nc.gpsimd.tensor_tensor(X[:, 0, :], Y[:, 0, :], ln_gb[:, 0, :], ALU.mult).then_inc(x_by_g[0], 1)
                pool.wait_ge(x_by_g[0], n + 1)
                nc.gpsimd.tensor_tensor(X[:, 0, :], X[:, 0, :], ln_gb[:, 1, :], ALU.add).then_inc(x_updated[0], 1)

            with pool.Fori(0, DEPTH) as l:
                n2 = pool.snap(l * 2)
                for t in range(TT):
                    pool.wait_ge(x_updated[t], n2 + 1)
                nc.gpsimd.tensor_tensor(stat[:, 76:77], half_neg[:, 0:1], half_neg[:, 1:2], ALU.add)
                nc.gpsimd.tensor_scalar(X[:, :, :], X[:, :, :], ALPHA, 0.0, ALU.mult, ALU.add).then_inc(residual_ready, 1)
                with pool.Fori(0, NJ) as j:
                    pool.wait_ge(gn_var_eps, l * NJ + j + 1)
                    nc.gpsimd.tensor_tensor(rs_gn, ve_gn, half_neg, ALU.pow).then_inc(gn_rstd, 1)
                update_x(n2, l * 32 + 16)
                for t in range(TT):
                    pool.wait_ge(x_updated[t], n2 + 2)
                nc.gpsimd.tensor_tensor(stat[:, 77:78], half_neg[:, 0:1], half_neg[:, 1:2], ALU.add)
                nc.gpsimd.tensor_scalar(X[:, :, :], X[:, :, :], ALPHA, 0.0, ALU.mult, ALU.add).then_inc(x_scaled, 1)
                pool.wait_ge(x_scaled, l + 1)
                pool.wait_ge(ple_ready, l * NJ + NJ)
                nc.gpsimd.tensor_tensor(X[:, :, :], X[:, :, :], ple, ALU.add).then_inc(residual_ready, 1)
                update_x(n2 + 1, l * 32 + 32)

        @block.tensor
        def _(pe):
            mm = nc.tensor.matmul

            def split_product(dst, st_hi, st_lo, mv_hi, mv_lo, start, stop):
                mm(dst, st_hi, mv_hi, start=start, stop=False)
                mm(dst, st_hi, mv_lo, start=False, stop=False)
                return mm(dst, st_lo, mv_hi, start=False, stop=stop)

            def weights_ready(c0, c):
                pe.wait_ge(lo_ready, c0 + c + 1 + RING)

            def transposed(c0, c, b, src_hi, src_lo, k0=0, start=True, stop=True):
                weights_ready(c0, c)
                s = c % RING
                for m in range(2):
                    for k in range(KT):
                        o = k * CH + m * P
                        ins = split_product(bank[b][:, m * SEQ:(m + 1) * SEQ], w_hi[:, s, o:o + P], w_lo[:, s, o:o + P],
                                            src_hi[:, k0 + k, :], src_lo[:, k0 + k, :],
                                            start and k == 0, stop and k == KT - 1 and (start or m == 1))
                ins.then_inc(chunk_done, 1)

            def by_token(c0, c, b, m=None):
                weights_ready(c0, c)
                s = c % RING
                for t in range(TT):
                    if m is not None:
                        pe.wait_ge(xT_lo_ready, m * 4 + 2 * t + 2)
                    for k in range(KT):
                        ins = split_product(bank[b][:, t * CH:(t + 1) * CH],
                                            xT_hi[:, k, t * P:(t + 1) * P], xT_lo[:, k, t * P:(t + 1) * P],
                                            w_hi[:, s, k * CH:(k + 1) * CH], w_lo[:, s, k * CH:(k + 1) * CH],
                                            k == 0, k == KT - 1)
                ins.then_inc(chunk_done, 1)

            def clear(dst):
                mm(dst, zero_r[:, 0:P], zero_r[:, :], start=True, stop=False)

            def from_mid(c0, c, n, last=False):
                pe.wait_ge(mid_lo_ready, n)
                weights_ready(c0, c)
                s = c % RING
                for t in range(TT):
                    for h in range(2):
                        for k in range(2):
                            o = k * D + h * 512
                            ins = split_product(acc[2 * t + h][:, :],
                                                mid_hi[:, k, t * P:(t + 1) * P], mid_lo[:, k, t * P:(t + 1) * P],
                                                w_hi[:, s, o:o + 512], w_lo[:, s, o:o + 512], False, last and k == 1)
                        if last and 2 * t + h < 3:
                            ins.then_inc(acc_part_done, 1)
                ins.then_inc(chunk_done, 1)

            def transpose_y(n):
                for t in range(TT):
                    pe.wait_ge(ln_y, n * TT + t + 1)
                    for k in range(KT):
                        ins = nc.tensor.transpose(acc[2 * t + k // 4][:, (k % 4) * P:(k % 4 + 1) * P],
                                                  Y[:, t, k * P:(k + 1) * P], ident)
                        if k % 4 == 3:
                            ins.then_inc(lnT_done, 1)

            with pe.Fori(0, DEPTH) as l:
                with pe.Fori(0, NJ) as j:
                    it = pe.snap(l * NJ + j)
                    it2 = pe.snap(it * 2)
                    c0 = pe.snap(l * C_LAYER + j * C_MIX)
                    used = [pe.snap(l * USES[b] + j * 5) for b in range(3)]

                    def scores(a):
                        for g in range(NG):
                            mm(acc[0][:, g * P:(g + 1) * P], qk[:, 2 * g, a, 0:P], qk[:, 2 * g + 1, a, 0:P],
                               start=True, stop=True)
                        for g in range(NG):
                            ins = mm(acc[1 + g // 2][:, (g % 2) * SEQ:(g % 2 + 1) * SEQ],
                                     qk[:, 2 * g, a, P:SEQ], qk[:, 2 * g + 1, a, :], start=True, stop=True)
                        ins.then_inc(scores_done, 1)

                    def transpose_prob(a):
                        pe.wait_ge(prob_ready, it2 + a + 1)
                        for g in range(NG):
                            for o, src in enumerate((g * P, 384 + g * 256, 384 + g * 256 + P)):
                                ins = nc.tensor.transpose(acc[g][:, o * P:(o + 1) * P], prob[:, src:src + P], ident)
                        ins.then_inc(probT_done, 1)

                    def attend(a):
                        for g in range(NG):
                            mm(acc[a][:, 0:SEQ], att_v[:, g, 0, a * P:(a + 1) * P], probT[:, a, g, 0:SEQ],
                               start=(g == 0), stop=False)
                            ins = mm(acc[a][:, P:SEQ], att_v[:, g, 1, a * P:(a + 1) * P], probT[:, a, g, SEQ:384],
                                     start=False, stop=(g == NG - 1))
                        ins.then_inc(pv_done, 1)

                    for c in range(C_MIX):
                        b = c % 3
                        pe.wait_ge(bank_read[b], used[b] + (c // 3 + 1))
                        if c in (0, 9, 10, 11, 12):
                            by_token(c0, c, b, l * 2 if c == 0 else None)
                        else:
                            transposed(c0, c, b, xT_hi, xT_lo)
                        if c == 7:
                            pe.wait_ge(bank_read[0], used[0] + 4)
                            pe.wait_ge(attn_lo_ready, it2 + 2)
                            pe.wait_ge(ret_affine, it + 1)
                            scores(0)
                        if c == 10:
                            pe.wait_ge(const_in, 16)
                            pe.wait_ge(roped_ready, it2 + 2)
                            for h in range(2):
                                mm(acc[3][:, 0:SEQ], roped[:, 1, h, 0:P], roped[:, 0, h, :], start=(h == 0), stop=(h == 1))
                            for h in range(2):
                                ins = mm(acc[3][:, SEQ:384], roped[:, 1, h, P:SEQ], roped[:, 0, h, P:SEQ],
                                         start=(h == 0), stop=(h == 1))
                            ins.then_inc(ret_scores_done, 1)
                            transpose_prob(0)
                        if c == 11:
                            pe.wait_ge(probT_copied, it2 + 1)
                            scores(1)
                        if c == 12:
                            pe.wait_ge(decayed_ready, it + 1)
                            pe.wait_ge(bank_read[0], used[0] + 5)
                            pe.wait_ge(bank_read[3], l * USES[3] + j + 1)
                            mm(bank[3][:, :], decayed[:, 0:P], rv[:, 0, :], start=True, stop=True)
                            mm(acc[3][:, :], decayed[:, P:SEQ], rv[:, 0, :], start=True, stop=False)
                            mm(acc[3][:, :], decayed[:, SEQ:384], rv[:, 1, :], start=False, stop=True)\
                                .then_inc(ret_av_done, 1)
                        if c == 13:
                            transpose_prob(1)
                    pe.wait_ge(probT_copied, it2 + 2)
                    pe.wait_ge(bank_read[0], used[0] + 6)
                    attend(0)
                    attend(1)
                    pe.wait_ge(ret_y_ready, it + 1)
                    for t in range(TT):
                        for k in range(4):
                            ins = nc.tensor.transpose(acc[2 + k // 2][:, (k % 2) * SEQ + t * P:(k % 2) * SEQ + (t + 1) * P],
                                                      ret_y[:, t, k * P:(k + 1) * P], ident)
                    ins.then_inc(ret_yT_done, 1)

                def gate(c0, c, b, j):
                    pe.wait_ge(bank_read[b], l * USES[b] + j + (U_MERGE[b] + 1))
                    transposed(c0, c, b, xT_hi, xT_lo)

                def mixers(c0, c, j):
                    pe.wait_ge(bank_read[2], l * USES[2] + j + (U_MERGE[2] + 1))
                    clear(bank[2][:, :])
                    transposed(c0, c, 2, ret_hi, ret_lo, 0, start=False, stop=False)
                    transposed(c0, c + 1, 2, ret_hi, ret_lo, KT, start=False)
                    pe.wait_ge(bank_read[3], l * USES[3] + j + (U_MERGE[3] + 1))
                    transposed(c0, c + 2, 3, attn_hi, attn_lo)

                c0 = pe.snap(l * C_LAYER + C_MERGE)
                gate(c0, 0, 0, 0)
                gate(c0, 1, 1, 0)
                pe.wait_ge(ret_lo_ready, l * NJ + NJ)
                pe.wait_ge(attn_lo_ready, l * (2 * NJ) + 2 * NJ + 2)
                pe.wait_ge(ret_affine, l * NJ + NJ + 1)
                pe.wait_ge(zeros_set, 1)
                for a in range(4):
                    clear(acc[a][:, :])
                mixers(c0, 2, 0)
                with pe.Fori(0, NJ - 1) as j:
                    c0 = pe.snap(l * C_LAYER + C_MERGE + j * 6)
                    gate(c0, 5, 0, j + 1)
                    from_mid(c0, 6, l * (NJ + NF) + j + 1)
                    gate(c0, 7, 1, j + 1)
                    mixers(c0, 8, j + 1)
                c0 = pe.snap(l * C_LAYER + C_PLE)
                from_mid(c0, -1, l * (NJ + NF) + NJ, last=True)

                for u in range(2):
                    weights_ready(c0, u)
                    for t in range(TT):
                        b = 2 * u + t
                        pe.wait_ge(bank_read[b], l * USES[b] + (U_PLE[b] + 1))
                        for k in range(2):
                            o = 1024 + k * SEQ + t * P
                            ins = split_product(bank[b][:, :], w_hi[:, u, o:o + P], w_lo[:, u, o:o + P],
                                                w_hi[:, u, k * 512:(k + 1) * 512], w_lo[:, u, k * 512:(k + 1) * 512],
                                                k == 0, k == 1)
                    ins.then_inc(chunk_done, 1)
                transpose_y(l * 2)
                for j in range(NJ):
                    pe.wait_ge(bank_read[j], l * USES[j] + (U_PLE[j] + 2))
                    by_token(c0, 2 + j, j, l * 2 + 1 if j == 0 else None)

                def up(c0, c, half, i):
                    pe.wait_ge(bank_read[half], l * USES[half] + i + (U_MLP[half] + 1))
                    transposed(c0, c, half, xT_hi, xT_lo)

                c0 = pe.snap(l * C_LAYER + C_MLP)
                for a in range(4):
                    clear(acc[a][:, :])
                up(c0, 0, 0, 0)
                up(c0, 1, 1, 0)
                with pe.Fori(0, NF - 1) as i:
                    c0 = pe.snap(l * C_LAYER + C_MLP + i * 3)
                    up(c0, 2, 0, i + 1)
                    up(c0, 3, 1, i + 1)
                    from_mid(c0, 4, l * (NJ + NF) + i + (NJ + 1))
                c0 = pe.snap(l * C_LAYER + C_LAYER)
                from_mid(c0, -1, l * (NJ + NF) + (NJ + NF), last=True)
                with pe.If(DEPTH - 1 - l):
                    transpose_y(l * 2 + 1)


def constant_table():
    t = np.zeros((P, NCC), np.float64)
    q = np.arange(P)[:, None]
    k = np.arange(2 * P)[None, :]
    dist = q + P - k
    for g, (window, dilation) in enumerate(GROUPS):
        ok = (dist >= 0) & (dist <= window) & (dist % dilation == 0)
        t[:, CC_MASK + g * 256:CC_MASK + (g + 1) * 256] = np.where(ok, 0.0, MASKED)
    rel = k - q
    for h in range(RH):
        log_gamma = np.log1p(-2.0 ** (-5.0 - h))
        t[:, CC_DEC + h * 256:CC_DEC + (h + 1) * 256] = np.where(
            rel >= 0, np.exp(log_gamma * np.maximum(rel, 0)), 0.0) * RET_SCALE
    t[:, CC_ID:CC_ID + P] = np.eye(P)
    t = t.astype(np.float32)
    t[:, CC_FREQ] = np.power(np.float32(10000.0), -np.arange(P, dtype=np.float32) / np.float32(P))
    return t


def kernel(**inputs):
    import concourse.bacc as _bacc
    from concourse.bass_utils import run_bass_kernel_spmd as _run

    a = {n: np.ascontiguousarray(v) for n, v in inputs.items()}

    def by_feature(v):
        return v.reshape(DEPTH, -1, P).transpose(0, 2, 1)

    feature_params = np.concatenate(
        [by_feature(a["conv_w"][:, i]) for i in range(3)] +
        [by_feature(a[n]) for n in ("conv_b", "ret_gn_g", "ret_gn_b", "ln1_g", "ln1_b", "ln2_g", "ln2_b")], axis=2)
    wp = a["w_ple_proj"].reshape(DEPTH, 2, P, 2, 512).transpose(0, 3, 2, 1, 4).reshape(DEPTH, 2, P, 1024)
    pt = a["p"].reshape(DEPTH, SEQ, 2, P).transpose(0, 3, 2, 1).reshape(DEPTH, 1, P, 2 * SEQ)
    arrays = {
        "x": a["x"].reshape(SEQ, D), "xT": a["x"].reshape(SEQ, D).T, "positions": a["positions"],
        "w_in": a["w_in"], "w_attn_proj": a["w_attn_proj"], "w_ret_proj": a["w_ret_proj"], "w_out": a["w_out"],
        "w_up": a["w_up"], "w_down": a["w_down"], "w_ple_gate": a["w_ple_gate"],
        "ple_operands": np.concatenate([wp, np.repeat(pt, 2, axis=1)], axis=3),
        "ln_rows": np.concatenate([a["ln1_g"], a["ln1_b"], a["ln2_g"], a["ln2_b"]], axis=1),
        "feature_params": feature_params, "constants": constant_table(),
    }
    arrays = {n: np.ascontiguousarray(v) for n, v in arrays.items()}
    nc = _bacc.Bacc("TRN2", target_bir_lowering=False, num_devices=1, dynamic_dma_scratch_size=1024)
    aps = [nc.dram_tensor(n, v.shape, mybir.dt.from_np(v.dtype), kind="ExternalInput").ap() for n, v in arrays.items()]
    out = nc.dram_tensor("out", (SEQ, D), F32, kind="ExternalOutput").ap()
    program(nc, *aps, out)
    r = _run(nc, [arrays], core_ids=[0])
    return r.results[0]["out"].reshape(1, SEQ, D)
```

```python
from contextlib import ExitStack

import concourse.bass as bass
import numpy as np
from concourse import mybir

F32 = mybir.dt.float32
F32R = mybir.dt.float32r
I32 = mybir.dt.int32
ACT = mybir.ActivationFunctionType
ALU = mybir.AluOpType
AX = mybir.AxisListType

P = 128
D = 1024
SEQ = 256
DEPTH = 2
TT = SEQ // P
KT = D // P
HEADS = 8
GROUPS = ((128, 1), (512, 4), (2048, 16))
NG = len(GROUPS)
RH = 4
RV = 512
D_FF = 2816
PLE = 256
ALPHA = (2 * DEPTH) ** 0.25
LN_EPS = 1e-5
GN_EPS = 1e-6
ATT_SCALE = float(P) ** -0.5
RET_SCALE = 256.0 ** -0.5
MASKED = -1e30

CH = 256
CE = KT * CH
RING = 3
RQ0 = NG * 3 * D
RK0, RV0, RG0 = RQ0 + D, RQ0 + 2 * D, RQ0 + 4 * D
GA0, GR0 = RQ0 + 6 * D, RQ0 + 7 * D

NJ = 4
C_MIX = 15
C_MERGE = NJ * C_MIX
C_PLE = C_MERGE + 6 * NJ
NF = D_FF // CH
C_MLP = C_PLE + 6
C_LAYER = C_MLP + 3 * NF
assert C_LAYER % RING == 0 and C_MERGE % RING == 0 and C_PLE % RING == 0 and C_MLP % RING == 0

CE_PLE = 2 * 512 + 2 * SEQ

USES = (20 + 4 + 2 + NF, 20 + 4 + 2 + NF, 20 + 4 + 2, 4 + 4 + 2)
U_MERGE = (20, 20, 20, 4)
U_PLE = (24, 24, 24, 8)
U_MLP = (26, 26, 26, 10)

NB = 2 * D_FF // P
PC_CW, PC_CB = 0, 3 * NB
PC_GG = PC_CB + NB
PC_GB = PC_GG + 16
PC_LN = PC_GB + 16
NPC = PC_LN + 4 * KT

CC_MASK = 0
CC_DEC = CC_MASK + NG * 256
CC_ID = CC_DEC + RH * 256
CC_FREQ = CC_ID + P
NCC = CC_FREQ + 1

TWO_PI = 2.0 * np.pi
C1 = 6.28125
C2 = float(np.float32(np.floor((TWO_PI - C1) * 2.0 ** 21) / 2.0 ** 21))
C3 = float(np.float32(TWO_PI - C1 - C2))
ROUND = 12582912.0
PI_IN = 3.1415925


def program(nc, x, xT, positions, w_in, w_attn_proj, w_ret_proj, w_out, w_up, w_down,
            w_ple_gate, ple_operands, ln_rows, feature_params, constants, out):
    ctx = ExitStack()
    with ctx:
        def sb(name, shape, dt=F32):
            return ctx.enter_context(nc.sbuf_tensor(name, shape, dt))

        def sem(name):
            return ctx.enter_context(nc.semaphore(name))

        raw = sb("raw", [P, RING, CE])
        w_hi = sb("w_hi", [P, RING, CE], F32R)
        w_lo = sb("w_lo", [P, RING, CE], F32R)
        X = sb("X", [P, TT, D])
        xT_hi = sb("xT_hi", [P, KT, SEQ], F32R)
        xT_lo = sb("xT_lo", [P, KT, SEQ], F32R)
        attn_hi = sb("attn_hi", [P, HEADS, SEQ], F32R)
        attn_lo = sb("attn_lo", [P, HEADS, SEQ], F32R)
        ret_hi = sb("ret_hi", [P, 16, SEQ], F32R)
        ret_lo = sb("ret_lo", [P, 16, SEQ], F32R)
        mid_hi = sb("mid_hi", [P, 2, 2, SEQ], F32R)
        mid_lo = sb("mid_lo", [P, 2, 2, SEQ], F32R)
        const = sb("const", [P, NCC])
        feat = sb("feat", [P, NPC])
        cosT = sb("cosT", [P, SEQ])
        sinT = sb("sinT", [P, SEQ])
        stat = sb("stat", [P, 96])
        decayed_hi = sb("decayed_hi", [P, 384], F32R)
        decayed_lo = sb("decayed_lo", [P, 384], F32R)
        zero_r = sb("zero_r", [P, 512], F32R)
        scratch = sb("scratch", [P, 13568])

        def view(start, shape):
            n = int(np.prod(shape))
            v = scratch[:, start:start + n]
            if len(shape) == 2:
                v = v.rearrange("p (a b) -> p a b", a=shape[0])
            if len(shape) == 3:
                v = v.rearrange("p (a b c) -> p a b c", a=shape[0], b=shape[1])
            return v

        rv_hi = mid_hi[:, :, :, :].rearrange("p s k t -> p (s k t)").rearrange("p (t n) -> p t n", t=TT)
        rv_lo = mid_lo[:, :, :, :].rearrange("p s k t -> p (s k t)").rearrange("p (t n) -> p t n", t=TT)
        qk = view(0, (6, 2, SEQ))
        att_v = view(3072, (NG, TT, CH))
        prob = view(4608, (1152,))
        probT = view(5760, (2, NG, 384))
        roped = view(8064, (2, 2, SEQ))
        rope_c = view(9088, (2, SEQ))
        rope_s = view(9600, (2, SEQ))
        decayed = view(11136, (384,))
        ret_y = view(11520, (TT, RV))
        ret_t = view(9088, (4, SEQ))
        silu = view(12544, (4, SEQ))
        ln_gb = view(0, (2, D))
        Y = view(2048, (TT, D))
        xT_f = view(4096, (KT, SEQ))
        ple = view(6144, (TT, D))
        sig = view(8192, (2, 512))
        prod_r = view(9216, (512,))
        prod_a = view(9728, (512,))
        mid = view(10240, (2, SEQ))
        hpad = view(10752, (4, 258))
        conv = view(11784, (4, SEQ))
        ple_sig = view(12808, (512,))

        mask = const[:, CC_MASK:CC_DEC].rearrange("p (g k) -> p g k", g=NG)
        decay = const[:, CC_DEC:CC_ID].rearrange("p (h k) -> p h k", h=RH)
        ident = const[:, CC_ID:CC_ID + P]

        st_gn = stat[:, 0:12]
        mv_gn = stat[:, 12:16].rearrange("p (t s) -> p t s", t=TT)
        ve_gn = stat[:, 16:18]
        rs_gn = stat[:, 18:20]
        st_ln = stat[:, 20:44].rearrange("p (t s) -> p t s", t=TT)
        mv_ln = stat[:, 44:48].rearrange("p (t s) -> p t s", t=TT)
        ve_ln = stat[:, 48:50]
        rs_ln = stat[:, 50:52]
        neg_max = stat[:, 52:54]
        row_sum = stat[:, 54:56]
        row_inv = stat[:, 56:58]
        row_max = stat[:, 58:60]
        half_neg = stat[:, 60:62]

        bank = [ctx.enter_context(nc.psum_tensor(f"bank{i}", [P, 512], F32)) for i in range(4)]
        acc = [ctx.enter_context(nc.psum_tensor(f"acc{i}", [P, 512], F32)) for i in range(4)]

        raw_loaded = [sem(f"raw_loaded{s}") for s in range(RING)]
        hi_ready = sem("hi_ready")
        lo_ready = sem("lo_ready")
        chunk_done = sem("chunk_done")
        bank_read = [sem(f"bank_read{i}") for i in range(4)]
        const_in, angle_in, x_in, feat_in, rows_in, stored = (sem(n) for n in (
            "const_in", "angle_in", "x_in", "feat_in", "rows_in", "stored"))
        xT_in = [sem(f"xT_in{t}") for t in range(TT)]
        angle_step, rotary_ready = sem("angle_step"), sem("rotary_ready")
        exponent_set, zeros_set, hpad_zeroed = sem("exponent_set"), sem("zeros_set"), sem("hpad_zeroed")
        xT_hi_ready, xT_lo_ready = sem("xT_hi_ready"), sem("xT_lo_ready")
        scores_done, scores_masked, row_max_ready, neg_max_ready = (sem(n) for n in (
            "scores_done", "scores_masked", "row_max_ready", "neg_max_ready"))
        exp_done, inv_ready, prob_ready = sem("exp_done"), sem("inv_ready"), sem("prob_ready")
        probT_done, probT_copied, pv_done = sem("probT_done"), sem("probT_copied"), sem("pv_done")
        attn_hi_ready, attn_lo_ready = sem("attn_hi_ready"), sem("attn_lo_ready")
        rope_products, roped_ready = sem("rope_products"), sem("roped_ready")
        rv_hi_ready = sem("rv_hi_ready")
        ret_scores_done, decayed_ready, ret_av_done = sem("ret_scores_done"), sem("decayed_ready"), sem("ret_av_done")
        decayed_hi_ready, decayed_lo_ready = sem("decayed_hi_ready"), sem("decayed_lo_ready")
        gn_stats, gn_mean_var, gn_var_eps, gn_rstd, ret_y_ready = (sem(n) for n in (
            "gn_stats", "gn_mean_var", "gn_var_eps", "gn_rstd", "ret_y_ready"))
        ret_yT_done, ret_affine, ret_gated = sem("ret_yT_done"), sem("ret_affine"), sem("ret_gated")
        ret_hi_ready, ret_lo_ready = sem("ret_hi_ready"), sem("ret_lo_ready")
        mid_ready, mid_hi_ready, mid_lo_ready = sem("mid_ready"), sem("mid_hi_ready"), sem("mid_lo_ready")
        acc_part_done = sem("acc_part_done")
        ln_sum, ln_stats, ln_mean_var, ln_var_eps, ln_rstd, ln_y = (sem(n) for n in (
            "ln_sum", "ln_stats", "ln_mean_var", "ln_var_eps", "ln_rstd", "ln_y"))
        lnT_done = sem("lnT_done")
        xT_f_ready = [sem(f"xT_f_ready{h}") for h in range(2)]
        x_by_g = [sem(f"x_by_g{t}") for t in range(TT)]
        x_updated = [sem(f"x_updated{t}") for t in range(TT)]
        x_scaled, residual_ready = sem("x_scaled"), sem("residual_ready")
        ple_ready = sem("ple_ready")
        conv_first, conv_ready, gelu_ready = sem("conv_first"), sem("conv_ready"), sem("gelu_ready")

        block = ctx.enter_context(nc.Block())

        @block.sync
        def _(sp):
            def load(c0, c, src, width=CE):
                s = c % RING
                dst = raw[:, s, 0:width]
                if len(src.shape) == 3:
                    dst = dst.rearrange("p (k n) -> p k n", k=src.shape[1])
                sp.wait_ge(lo_ready, c0 + c + 1)
                sp.dma_start(dst, src).then_inc(raw_loaded[s], 16)

            def part(w, l, k0, nk, n0, n):
                v = w.rearrange("l (k p) n -> l p k n", p=P)
                return v[bass.ds(l, 1), :, bass.ds(k0, nk), bass.ds(n0, n)].rearrange("l p k n -> (l p) k n")

            sp.dma_start(const[:, CC_ID:NCC], constants[:, CC_ID:NCC]).then_inc(angle_in, 16)
            sp.dma_start(xT_f[:, :, 0:P], xT.rearrange("(k p) t -> p k t", p=P)[:, :, 0:P]).then_inc(xT_in[0], 16)
            with sp.Fori(0, DEPTH) as l:
                with sp.Fori(0, NJ) as j:
                    c0 = sp.snap(l * C_LAYER + j * C_MIX)
                    load(c0, 0, part(w_in, l, 0, KT, j * RV + RV0, CH))
                    for c in range(6):
                        load(c0, 1 + c, part(w_in, l, 0, KT, j * CH + (3 * (c // 2) + c % 2) * D, CH))
                    load(c0, 7, part(w_in, l, 0, KT, j * CH + RQ0, CH))
                    load(c0, 8, part(w_in, l, 0, KT, j * CH + RK0, CH))
                    load(c0, 9, part(w_in, l, 0, KT, j * RV + RV0 + CH, CH))
                    for g in range(NG):
                        load(c0, 10 + g, part(w_in, l, 0, KT, j * CH + (3 * g + 2) * D, CH))
                    for u in range(2):
                        load(c0, 13 + u, part(w_in, l, 0, KT, j * RV + RG0 + u * CH, CH))
                c0 = sp.snap(l * C_LAYER + C_MERGE)
                load(c0, 0, part(w_in, l, 0, KT, GA0, CH))
                load(c0, 1, part(w_in, l, 0, KT, GR0, CH))
                load(c0, 2, part(w_ret_proj, l, 0, KT, 0, CH))
                load(c0, 3, part(w_ret_proj, l, KT, KT, 0, CH))
                load(c0, 4, part(w_attn_proj, l, 0, KT, 0, CH))
                with sp.Fori(0, NJ - 2) as j:
                    c0 = sp.snap(l * C_LAYER + C_MERGE + j * 6)
                    load(c0, 5, part(w_in, l, 0, KT, j * CH + GA0 + CH, CH))
                    load(c0, 6, part(w_out, l, j * 2, 2, 0, D))
                    load(c0, 7, part(w_in, l, 0, KT, j * CH + GR0 + CH, CH))
                    load(c0, 8, part(w_ret_proj, l, 0, KT, j * CH + CH, CH))
                    load(c0, 9, part(w_ret_proj, l, KT, KT, j * CH + CH, CH))
                    load(c0, 10, part(w_attn_proj, l, 0, KT, j * CH + CH, CH))
                c0 = sp.snap(l * C_LAYER + C_PLE)
                load(c0, -7, part(w_in, l, 0, KT, GA0 + (NJ - 1) * CH, CH))
                load(c0, -6, part(w_in, l, 0, KT, GR0 + (NJ - 1) * CH, CH))
                load(c0, -5, part(w_ret_proj, l, 0, KT, (NJ - 1) * CH, CH))
                load(c0, -4, part(w_ret_proj, l, KT, KT, (NJ - 1) * CH, CH))
                load(c0, -3, part(w_attn_proj, l, 0, KT, (NJ - 1) * CH, CH))
                load(c0, -2, part(w_out, l, 2 * NJ - 4, 2, 0, D))
                load(c0, -1, part(w_out, l, 2 * NJ - 2, 2, 0, D))
                for u in range(2):
                    load(c0, u, ple_operands[bass.ds(l, 1), u, :, :].rearrange("l p n -> (l p) n"), CE_PLE)
                for j in range(NJ):
                    load(c0, 2 + j, part(w_ple_gate, l, 0, KT, j * CH, CH))
                c0 = sp.snap(l * C_LAYER + C_MLP)
                load(c0, 0, part(w_up, l, 0, KT, 0, CH))
                load(c0, 1, part(w_up, l, 0, KT, D_FF, CH))
                with sp.Fori(0, NF - 1) as i:
                    c0 = sp.snap(l * C_LAYER + C_MLP + i * 3)
                    load(c0, 2, part(w_up, l, 0, KT, i * CH + CH, CH))
                    load(c0, 3, part(w_up, l, 0, KT, i * CH + D_FF + CH, CH))
                    load(c0, 4, part(w_down, l, i * 2, 2, 0, D))
                c0 = sp.snap(l * C_LAYER + C_MLP + 3 * NF)
                load(c0, -1, part(w_down, l, 2 * NF - 2, 2, 0, D))
            for t in reversed(range(TT)):
                sp.wait_ge(x_updated[t], 2 * DEPTH + 1)
                sp.dma_start(out[t * P:(t + 1) * P, :], X[:, t, :]).then_inc(stored, 16)
            sp.wait_ge(stored, 16 * TT)

        @block.scalar
        def _(act):
            def to_hi(c0, r0, c):
                s = c % RING
                act.wait_ge(raw_loaded[s], r0 + 16 * (c // RING + 1))
                act.wait_ge(chunk_done, c0 + c + 1)
                nc.scalar.activation(w_hi[:, s, :], raw[:, s, :], ACT.Copy).then_inc(hi_ready, 1)

            def copy_out(c0, c, b, dst, scale=1.0, func=ACT.Copy):
                src = bank[b][:, :]
                if len(dst.shape) == 3:
                    src = src.rearrange("p (a b) -> p a b", a=dst.shape[1])
                act.wait_ge(chunk_done, c0 + c + 1 + RING)
                nc.scalar.activation(dst, src, func, scale=scale).then_inc(bank_read[b], 1)

            def x_high(n, w, t):
                g0, b0 = PC_LN + 2 * w * KT, PC_LN + (2 * w + 1) * KT
                act.wait_ge(lnT_done, n * 4 + 2 * t + 2)
                for k in range(4, 8):
                    ins = nc.scalar.activation(xT_f[:, k, t * P:(t + 1) * P], acc[2 * t + 1][:, (k - 4) * P:(k - 3) * P],
                                               ACT.Identity, scale=feat[:, g0 + k:g0 + k + 1],
                                               bias=feat[:, b0 + k:b0 + k + 1])
                ins.then_inc(xT_f_ready[1], 1)
                for h in range(2):
                    act.wait_ge(xT_f_ready[h], n * TT + t + 1)
                    v = (slice(None), slice(4 * h, 4 * h + 4), slice(t * P, (t + 1) * P))
                    nc.scalar.activation(xT_hi[v], xT_f[v], ACT.Copy).then_inc(xT_hi_ready, 1)

            act.dma_start(sinT[:, :].bitcast(I32), positions.rearrange("a t -> (a t)").partition_broadcast(P))\
               .then_inc(angle_in, 16)
            for t in range(TT):
                act.wait_ge(xT_in[t], 16)
                if t == 0:
                    act.dma_start(xT_f[:, :, P:SEQ], xT.rearrange("(k p) t -> p k t", p=P)[:, :, P:SEQ])\
                       .then_inc(xT_in[1], 16)
                for h in range(2):
                    v = (slice(None), slice(4 * h, 4 * h + 4), slice(t * P, (t + 1) * P))
                    nc.scalar.activation(xT_hi[v], xT_f[v], ACT.Copy).then_inc(xT_hi_ready, 1)
                if t == 0:
                    to_hi(0, 0, 0)
            to_hi(0, 0, 1)
            act.dma_start(const[:, 0:CC_ID], constants[:, 0:CC_ID]).then_inc(const_in, 16)
            act.dma_start(X[:, :, :], x.rearrange("(t p) n -> p t n", p=P)).then_inc(x_in, 16)
            act.wait_ge(angle_step, 10)
            nc.scalar.activation(sinT[:, :], sinT[:, :], ACT.Sin).then_inc(rotary_ready, 1)
            nc.scalar.activation(cosT[:, :], cosT[:, :], ACT.Sin).then_inc(rotary_ready, 1)

            with act.Fori(0, DEPTH) as l:
                n2 = act.snap(l * 2)
                act.wait_ge(xT_lo_ready, n2 * 4 + 4)
                act.dma_start(feat[:, :], feature_params[bass.ds(l, 1), :, :].rearrange("l p n -> (l p) n"))\
                   .then_inc(feat_in, 16)
                with act.Fori(0, NJ) as j:
                    it = act.snap(l * NJ + j)
                    it2 = act.snap(it * 2)
                    c0 = act.snap(l * C_LAYER + j * C_MIX)
                    r0 = act.snap(l * (16 * C_LAYER // RING) + j * (16 * C_MIX // RING))

                    def exp(a):
                        act.wait_ge(neg_max_ready, it2 + a + 1)
                        nc.scalar.activation(prob[:, 0:384], prob[:, 0:384], ACT.Exp, bias=neg_max[:, 0:1],
                                             accum_out=row_sum[:, 0:1])
                        nc.scalar.activation(prob[:, 384:1152], prob[:, 384:1152], ACT.Exp, bias=neg_max[:, 1:2],
                                             accum_out=row_sum[:, 1:2]).then_inc(exp_done, 1)

                    def copy_probT(a):
                        act.wait_ge(probT_done, it2 + a + 1)
                        for g in range(NG):
                            ins = nc.scalar.activation(probT[:, a, g, :], acc[g][:, 0:384], ACT.Copy)
                        ins.then_inc(probT_copied, 1)

                    for c in range(C_MIX):
                        to_hi(c0, r0, c + 2)
                        if c in (0, 9):
                            u = c // 9
                            act.wait_ge(chunk_done, c0 + c + 1 + RING)
                            nc.scalar.activation(rv_hi[:, :, u * CH:(u + 1) * CH],
                                                 bank[0][:, :].rearrange("p (t n) -> p t n", t=TT),
                                                 ACT.Copy).then_inc(rv_hi_ready, 1)
                        if c == 1:
                            for t in range(TT):
                                act.wait_ge(x_updated[t], n2 + 1)
                        if c in range(1, 7):
                            copy_out(c0, c, c % 3, qk[:, c - 1, :, :], scale=ATT_SCALE if c % 2 == 1 else 1.0)
                        if c == 8:
                            exp(0)
                        if c == 11:
                            copy_probT(0)
                            act.wait_ge(decayed_ready, it + 1)
                            nc.scalar.activation(decayed_hi[:, :], decayed, ACT.Copy).then_inc(decayed_hi_ready, 1)
                        if c in (10, 11, 12):
                            copy_out(c0, c, c % 3, att_v[:, c - 10, :, :])
                        if c == 12:
                            exp(1)
                        if c == 14:
                            copy_probT(1)
                        if c in (13, 14):
                            copy_out(c0, c, c % 3, silu[:, 2 * (c - 13):2 * (c - 12), :], func=ACT.Silu)
                    for a in range(2):
                        act.wait_ge(pv_done, it2 + a + 1)
                        nc.scalar.activation(attn_hi[:, bass.ds(j * 2 + a, 1), :],
                                             acc[a][:, 0:SEQ].rearrange("p (a b) -> p a b", a=1),
                                             ACT.Copy).then_inc(attn_hi_ready, 1)
                    act.wait_ge(ret_yT_done, it + 1)
                    act.wait_ge(feat_in, l * 16 + 16)
                    for k in range(4):
                        ins = nc.scalar.activation(ret_t[:, k, :], acc[2 + k // 2][:, (k % 2) * SEQ:(k % 2 + 1) * SEQ],
                                                   ACT.Identity, scale=feat[:, bass.ds(j * 4 + (PC_GG + k), 1)],
                                                   bias=feat[:, bass.ds(j * 4 + (PC_GB + k), 1)])
                    ins.then_inc(ret_affine, 1)
                    act.wait_ge(ret_gated, it + 1)
                    nc.scalar.activation(ret_hi[:, bass.ds(j * 4, 4), :], ret_t, ACT.Copy).then_inc(ret_hi_ready, 1)

                c0 = act.snap(l * C_LAYER + C_MERGE)
                r0 = act.snap(l * (16 * C_LAYER // RING) + 16 * C_MERGE // RING)
                act.wait_ge(ret_lo_ready, l * NJ + NJ)
                act.dma_start(ln_gb, ln_rows[bass.ds(l, 1), 0:2 * D].rearrange("l n -> (l n)")
                              .partition_broadcast(P).rearrange("p (r n) -> p r n", r=2)).then_inc(rows_in, 16)
                nm = act.snap(l * (NJ + NF))

                def mid_high(n, slot=0):
                    act.wait_ge(mid_ready, n)
                    nc.scalar.activation(mid_hi[:, slot, :, :], mid, ACT.Copy).then_inc(mid_hi_ready, 1)

                for c in range(5):
                    to_hi(c0, r0, c + 2)
                    if c < 2:
                        copy_out(c0, c, c, sig[:, c, :], func=ACT.Sigmoid)
                mid_high(nm + 1)
                with act.Fori(0, NJ - 2) as j:
                    c0 = act.snap(l * C_LAYER + C_MERGE + j * 6)
                    r0 = act.snap(l * (16 * C_LAYER // RING) + 16 * C_MERGE // RING + j * 32)
                    nm = act.snap(l * (NJ + NF) + j)
                    for c in range(5, 11):
                        to_hi(c0, r0, c + 2)
                        if c == 5:
                            copy_out(c0, 5, 0, sig[:, 0, :], func=ACT.Sigmoid)
                        if c == 7:
                            copy_out(c0, 7, 1, sig[:, 1, :], func=ACT.Sigmoid)
                    mid_high(nm + 2)

                c0 = act.snap(l * C_LAYER + C_PLE)
                r0 = act.snap(l * (16 * C_LAYER // RING) + 16 * C_PLE // RING)
                for c in range(-7, -1):
                    to_hi(c0, r0, c + 2)
                    if c in (-7, -6):
                        copy_out(c0, c, c + 7, sig[:, c + 7, :], func=ACT.Sigmoid)
                mid_high(l * (NJ + NF) + NJ, slot=1)
                to_hi(c0, r0, 1)
                to_hi(c0, r0, 2)
                for u in range(2):
                    act.wait_ge(chunk_done, c0 + u + 1 + RING)
                    for t in range(TT):
                        nc.scalar.activation(ple[:, t, u * 512:(u + 1) * 512], bank[2 * u + t][:, :],
                                             ACT.Copy).then_inc(bank_read[2 * u + t], 1)
                    x_high(n2, 0, u)
                to_hi(c0, r0, 3)
                for j in range(NJ):
                    to_hi(c0, r0, 4 + j)
                    if j:
                        act.wait_ge(ple_ready, l * NJ + j)
                    copy_out(c0, 2 + j, j, ple_sig, func=ACT.Sigmoid)
                for t in range(TT):
                    act.wait_ge(x_updated[t], n2 + 2)
                act.dma_start(ln_gb, ln_rows[bass.ds(l, 1), 2 * D:4 * D].rearrange("l n -> (l n)")
                              .partition_broadcast(P).rearrange("p (r n) -> p r n", r=2)).then_inc(rows_in, 16)

                def take_h(c0, c, half, nm, i):
                    src = bank[half][:, :].rearrange("p (a b) -> p a b", a=2)
                    act.wait_ge(chunk_done, c0 + c + 1 + RING)
                    act.wait_ge(mid_ready, nm)
                    nc.scalar.activation(hpad[:, 2 * half:2 * half + 2, 2:2 + SEQ], src, ACT.Copy)
                    for b in range(2):
                        blk = half * (NB // 2) + b
                        ins = nc.scalar.activation(conv[:, 2 * half + b, :], src[:, b, :], ACT.Identity,
                                                   scale=feat[:, bass.ds(i * 2 + (PC_CW + 2 * NB + blk), 1)],
                                                   bias=feat[:, bass.ds(i * 2 + (PC_CB + blk), 1)])
                    ins.then_inc(bank_read[half], 1)

                def gelu(turn):
                    act.wait_ge(conv_ready, 2 * turn + 1)
                    nc.scalar.activation(conv[:, 0:2, :], conv[:, 0:2, :], ACT.Gelu_apprx_tanh).then_inc(gelu_ready, 1)

                c0 = act.snap(l * C_LAYER + C_MLP)
                r0 = act.snap(l * (16 * C_LAYER // RING) + 16 * C_MLP // RING)
                nm = act.snap(l * (NJ + NF) + NJ)
                to_hi(c0, r0, 2)
                take_h(c0, 0, 0, nm, 0)
                gelu(act.snap(l * NF))
                take_h(c0, 1, 1, nm, 0)
                with act.Fori(0, NF - 1) as i:
                    c0 = act.snap(l * C_LAYER + C_MLP + i * 3)
                    r0 = act.snap(l * (16 * C_LAYER // RING) + 16 * C_MLP // RING + i * 16)
                    next_turn = act.snap(l * NF + i + 1)
                    nm = act.snap(l * (NJ + NF) + NJ + i)
                    to_hi(c0, r0, 3)
                    to_hi(c0, r0, 4)
                    mid_high(nm + 1)
                    take_h(c0, 2, 0, nm + 1, i + 1)
                    to_hi(c0, r0, 5)
                    gelu(next_turn)
                    take_h(c0, 3, 1, nm + 1, i + 1)
                mid_high(l * (NJ + NF) + (NJ + NF), slot=1)
                with act.If(DEPTH - 1 - l):
                    c0 = act.snap(l * C_LAYER + C_LAYER)
                    r0 = act.snap(l * (16 * C_LAYER // RING) + 16 * C_LAYER // RING)
                    to_hi(c0, r0, 0)
                    to_hi(c0, r0, 1)
                    for t in range(TT):
                        x_high(n2 + 1, 1, t)

        @block.vector
        def _(dve):
            def to_lo(c0, c):
                s = c % RING
                dve.wait_ge(hi_ready, c0 + c + 1)
                nc.vector.tensor_tensor(w_lo[:, s, :], raw[:, s, :], w_hi[:, s, :].bitcast(F32),
                                        ALU.subtract).then_inc(lo_ready, 1)

            def mid_low(n, slot):
                dve.wait_ge(mid_hi_ready, n)
                nc.vector.tensor_tensor(mid_lo[:, slot, :, :], mid, mid_hi[:, slot, :, :].bitcast(F32),
                                        ALU.subtract).then_inc(mid_lo_ready, 1)

            def summed(n, c_end, q):
                t, h = q // 2, q % 2
                if q < 3:
                    dve.wait_ge(acc_part_done, n * 3 + q + 1)
                else:
                    dve.wait_ge(chunk_done, c_end + RING)
                nc.vector.tensor_tensor(Y[:, t, h * 512:(h + 1) * 512], X[:, t, h * 512:(h + 1) * 512],
                                        acc[q][:, :], ALU.add).then_inc(ln_sum, 1)
                dve.wait_ge(ln_sum, n * 4 + q + 1)
                ins = nc.vector.bn_stats(st_ln[:, t, h * 6:(h + 1) * 6], Y[:, t, h * 512:(h + 1) * 512])
                if h:
                    ins.then_inc(ln_stats, 1)

            def mean_and_variance(n, t):
                dve.wait_ge(ln_stats, n * TT + t + 1)
                nc.vector.memset(stat[:, 74:75], 0.0)
                nc.vector.bn_aggr(mv_ln[:, t, :], st_ln[:, t, :]).then_inc(ln_mean_var, 1)
                dve.wait_ge(ln_mean_var, n * TT + t + 1)
                nc.vector.tensor_scalar(ve_ln[:, t:t + 1], mv_ln[:, t, 1:2], LN_EPS, None, ALU.add)\
                  .then_inc(ln_var_eps, 1)

            def normalised(n, t):
                dve.wait_ge(ln_rstd, n * TT + t + 1)
                nc.vector.tensor_scalar(Y[:, t, :], Y[:, t, :], mv_ln[:, t, 0:1], rs_ln[:, t:t + 1],
                                        ALU.subtract, ALU.mult).then_inc(ln_y, 1)

            def layer_norm_start(n, c_end):
                dve.wait_ge(residual_ready, n + 1)
                summed(n, c_end, 0)
                summed(n, c_end, 1)
                mean_and_variance(n, 0)
                summed(n, c_end, 2)
                normalised(n, 0)
                summed(n, c_end, 3)
                mean_and_variance(n, 1)

            def x_low(m, t):
                for h in range(2):
                    dve.wait_ge(xT_hi_ready, m * 4 + 2 * t + h + 1)
                    v = (slice(None), slice(4 * h, 4 * h + 4), slice(t * P, (t + 1) * P))
                    nc.vector.tensor_tensor(xT_lo[v], xT_f[v], xT_hi[v].bitcast(F32), ALU.subtract)\
                      .then_inc(xT_lo_ready, 1)

            def x_transposed(n, w, t):
                g0, b0 = PC_LN + 2 * w * KT, PC_LN + (2 * w + 1) * KT
                dve.wait_ge(lnT_done, n * 4 + 2 * t + 1)
                for k in range(4):
                    ins = nc.vector.tensor_scalar(xT_f[:, k, t * P:(t + 1) * P], acc[2 * t][:, k * P:(k + 1) * P],
                                                  feat[:, g0 + k:g0 + k + 1], feat[:, b0 + k:b0 + k + 1],
                                                  ALU.mult, ALU.add)
                ins.then_inc(xT_f_ready[0], 1)

            def second_tile(n, rows):
                dve.wait_ge(rows_in, rows)
                dve.wait_ge(ln_y, n * TT + TT)
                nc.vector.tensor_tensor(X[:, 1, :], Y[:, 1, :], ln_gb[:, 0, :], ALU.mult).then_inc(x_by_g[1], 1)
                dve.wait_ge(x_by_g[1], n + 1)
                nc.vector.tensor_tensor(X[:, 1, :], X[:, 1, :], ln_gb[:, 1, :], ALU.add).then_inc(x_updated[1], 1)

            nc.vector.memset(stat[:, 64:65], 0.0).then_inc(lo_ready, 1)
            nc.vector.memset(stat[:, 65:66], 0.0).then_inc(chunk_done, RING)
            for b in range(4):
                nc.vector.memset(stat[:, 66 + b:67 + b], 0.0).then_inc(bank_read[b], 1)
            nc.vector.memset(stat[:, 70:71], 0.0).then_inc(attn_lo_ready, 2)
            nc.vector.memset(stat[:, 71:72], 0.0).then_inc(ret_affine, 1)
            nc.vector.memset(stat[:, 72:73], 0.0).then_inc(ret_hi_ready, 1)
            for t in range(TT):
                nc.vector.memset(stat[:, 78 + t:79 + t], 0.0).then_inc(x_updated[t], 1)
            nc.vector.memset(zero_r[:, :].bitcast(F32), 0.0).then_inc(zeros_set, 1)

            steps = [0]

            def angle(ins):
                steps[0] += 1
                ins.then_inc(angle_step, 1)
                dve.wait_ge(angle_step, steps[0])

            ang, turns = rope_c[:, 0, :], rope_c[:, 1, :]
            dve.wait_ge(angle_in, 32)
            angle(nc.vector.tensor_copy(cosT[:, :], sinT[:, :].bitcast(I32)))
            angle(nc.vector.tensor_scalar(ang, cosT[:, :], const[:, CC_FREQ:CC_FREQ + 1], None, ALU.mult))
            angle(nc.vector.tensor_scalar(turns, ang, 1.0 / TWO_PI, ROUND, ALU.mult, ALU.add))
            angle(nc.vector.tensor_scalar(turns, turns, ROUND, None, ALU.subtract))
            for part_of_2pi in (C1, C2, C3):
                angle(nc.vector.scalar_tensor_tensor(out=ang, in0=turns, scalar=-part_of_2pi, in1=ang,
                                                     op0=ALU.mult, op1=ALU.add))
            nc.vector.memset(stat[:, 73:74], 0.0).then_inc(lo_ready, RING - 1)
            angle(nc.vector.tensor_scalar(sinT[:, :], ang, PI_IN, -PI_IN, ALU.min, ALU.max))
            angle(nc.vector.scalar_tensor_tensor(out=turns, in0=sinT[:, :], scalar=-1.0, in1=sinT[:, :],
                                                 op0=ALU.mult, op1=ALU.max))
            angle(nc.vector.tensor_scalar(cosT[:, :], turns, -1.0, TWO_PI / 4, ALU.mult, ALU.add))

            x_low(0, 0)
            to_lo(0, 0)
            x_low(0, 1)
            to_lo(0, 1)

            with dve.Fori(0, DEPTH) as l:
                with dve.Fori(0, NJ) as j:
                    it = dve.snap(l * NJ + j)
                    it2 = dve.snap(it * 2)
                    c0 = dve.snap(l * C_LAYER + j * C_MIX)

                    def rotate(i):
                        b = i + 1
                        src = bank[b]
                        dve.wait_ge(chunk_done, c0 + 7 + i + 1 + RING)
                        if i == 0:
                            dve.wait_ge(rotary_ready, 2)
                            dve.wait_ge(ret_hi_ready, it + 1)
                        for h in range(2):
                            nc.vector.tensor_tensor(rope_c[:, h, :], src[:, h * SEQ:(h + 1) * SEQ], cosT[:, :], ALU.mult)
                        nc.vector.tensor_tensor(rope_s[:, 0, :], src[:, 0:SEQ], sinT[:, :], ALU.mult)\
                          .then_inc(rope_products, 1)
                        nc.vector.tensor_tensor(rope_s[:, 1, :], src[:, SEQ:2 * SEQ], sinT[:, :], ALU.mult)\
                          .then_inc(bank_read[b], 1)
                        dve.wait_ge(bank_read[b], l * USES[b] + j * 5 + 2 + 2)
                        nc.vector.tensor_tensor(roped[:, i, 0, :], rope_c[:, 0, :], rope_s[:, 1, :], ALU.subtract)
                        nc.vector.tensor_tensor(roped[:, i, 1, :], rope_s[:, 0, :], rope_c[:, 1, :], ALU.add)\
                          .then_inc(roped_ready, 1)
                        if i == 0:
                            dve.wait_ge(roped_ready, it2 + 1)

                    def mask_and_max(a):
                        if a == 0:
                            dve.wait_ge(const_in, 16)
                        dve.wait_ge(scores_done, it2 + a + 1)
                        nc.vector.tensor_tensor(prob[:, 0:384].rearrange("p (g k) -> p g k", g=NG),
                                                acc[0][:, 0:384].rearrange("p (g k) -> p g k", g=NG),
                                                mask[:, :, P:2 * P], ALU.add)
                        nc.vector.tensor_tensor(prob[:, 384:896].rearrange("p (g k) -> p g k", g=2),
                                                acc[1][:, :].rearrange("p (g k) -> p g k", g=2), mask[:, 0:2, :], ALU.add)
                        nc.vector.tensor_tensor(prob[:, 896:1152], acc[2][:, 0:256], mask[:, 2, :], ALU.add)\
                          .then_inc(scores_masked, 1)
                        dve.wait_ge(scores_masked, it2 + a + 1)
                        nc.vector.reduce_max(row_max[:, 0:1], prob[:, 0:384], AX.X)
                        nc.vector.reduce_max(row_max[:, 1:2], prob[:, 384:1152], AX.X).then_inc(row_max_ready, 1)
                        dve.wait_ge(row_max_ready, it2 + a + 1)
                        nc.vector.tensor_scalar(neg_max, row_max, -1.0, None, ALU.mult).then_inc(neg_max_ready, 1)

                    def normalise(a):
                        dve.wait_ge(exp_done, it2 + a + 1)
                        nc.vector.reciprocal(row_inv, row_sum).then_inc(inv_ready, 1)
                        dve.wait_ge(inv_ready, it2 + a + 1)
                        nc.vector.tensor_scalar(prob[:, 0:384], prob[:, 0:384], row_inv[:, 0:1], None, ALU.mult)
                        nc.vector.tensor_scalar(prob[:, 384:1152], prob[:, 384:1152], row_inv[:, 1:2], None, ALU.mult)\
                          .then_inc(prob_ready, 1)

                    for c in range(C_MIX):
                        if c == 0:
                            dve.wait_ge(lo_ready, c0 + 2 + RING)
                        to_lo(c0, c + 2)
                        if c in (0, 9):
                            u = c // 9
                            dve.wait_ge(rv_hi_ready, it2 + u + 1)
                            nc.vector.tensor_tensor(rv_lo[:, :, u * CH:(u + 1) * CH],
                                                    bank[0][:, :].rearrange("p (t n) -> p t n", t=TT),
                                                    rv_hi[:, :, u * CH:(u + 1) * CH].bitcast(F32), ALU.subtract)\
                              .then_inc(bank_read[0], 1)
                        if c == 7:
                            rotate(0)
                        if c == 8:
                            mask_and_max(0)
                            rotate(1)
                        if c == 9:
                            normalise(0)
                        if c == 11:
                            dve.wait_ge(ret_scores_done, it + 1)
                            nc.vector.tensor_tensor(decayed[:, 0:256].rearrange("p (a b) -> p a b", a=1),
                                                    acc[3][:, 0:256].rearrange("p (a b) -> p a b", a=1),
                                                    decay[:, bass.ds(j, 1), :], ALU.mult)
                            nc.vector.tensor_tensor(decayed[:, 256:384].rearrange("p (a b) -> p a b", a=1),
                                                    acc[3][:, 256:384].rearrange("p (a b) -> p a b", a=1),
                                                    decay[:, bass.ds(j, 1), 0:P], ALU.mult).then_inc(decayed_ready, 1)
                            dve.wait_ge(decayed_hi_ready, it + 1)
                            nc.vector.tensor_tensor(decayed_lo[:, :], decayed, decayed_hi[:, :].bitcast(F32),
                                                    ALU.subtract).then_inc(decayed_lo_ready, 1)
                        if c == 12:
                            mask_and_max(1)
                            normalise(1)
                        if c == 13:
                            dve.wait_ge(ret_av_done, it + 1)
                            for t, av in enumerate((bank[3], acc[3])):
                                ins = nc.vector.bn_stats(st_gn[:, t * 6:(t + 1) * 6], av[:, :])
                            ins.then_inc(gn_stats, 1)
                            dve.wait_ge(gn_stats, it + 1)
                            nc.vector.memset(stat[:, 75:76], 0.0)
                            for t in range(TT):
                                ins = nc.vector.bn_aggr(mv_gn[:, t, :], st_gn[:, t * 6:(t + 1) * 6])
                            ins.then_inc(gn_mean_var, 1)
                            dve.wait_ge(gn_mean_var, it + 1)
                            nc.vector.tensor_scalar(ve_gn, mv_gn[:, :, 1], GN_EPS, None, ALU.add).then_inc(gn_var_eps, 1)
                        if c == 14:
                            dve.wait_ge(gn_rstd, it + 1)
                            nc.vector.tensor_scalar(ret_y[:, 0, :], bank[3][:, :], mv_gn[:, 0, 0:1], rs_gn[:, 0:1],
                                                    ALU.subtract, ALU.mult).then_inc(bank_read[3], 1)
                            nc.vector.tensor_scalar(ret_y[:, 1, :], acc[3][:, :], mv_gn[:, 1, 0:1], rs_gn[:, 1:2],
                                                    ALU.subtract, ALU.mult).then_inc(ret_y_ready, 1)
                    for a in range(2):
                        dve.wait_ge(attn_hi_ready, it2 + a + 1)
                        nc.vector.tensor_tensor(attn_lo[:, bass.ds(j * 2 + a, 1), :],
                                                acc[a][:, 0:SEQ].rearrange("p (a b) -> p a b", a=1),
                                                attn_hi[:, bass.ds(j * 2 + a, 1), :].bitcast(F32),
                                                ALU.subtract).then_inc(attn_lo_ready, 1)
                    dve.wait_ge(ret_affine, it + 2)
                    nc.vector.tensor_tensor(ret_t, ret_t, silu, ALU.mult).then_inc(ret_gated, 1)
                    dve.wait_ge(ret_hi_ready, it + 2)
                    nc.vector.tensor_tensor(ret_lo[:, bass.ds(j * 4, 4), :], ret_t,
                                            ret_hi[:, bass.ds(j * 4, 4), :].bitcast(F32),
                                            ALU.subtract).then_inc(ret_lo_ready, 1)

                def merge(c0, cs, j, nm, slot=0):
                    dve.wait_ge(bank_read[1], l * USES[1] + j + (U_MERGE[1] + 2))
                    dve.wait_ge(chunk_done, c0 + cs[0] + 1 + RING)
                    nc.vector.tensor_tensor(prod_r, sig[:, 1, :], bank[2][:, :], ALU.mult).then_inc(bank_read[2], 1)
                    dve.wait_ge(chunk_done, c0 + cs[1] + 1 + RING)
                    nc.vector.tensor_tensor(prod_a, sig[:, 0, :], bank[3][:, :], ALU.mult).then_inc(bank_read[3], 1)
                    dve.wait_ge(bank_read[3], l * USES[3] + j + (U_MERGE[3] + 2))
                    nc.vector.tensor_tensor(mid, prod_r.rearrange("p (a b) -> p a b", a=2),
                                            prod_a.rearrange("p (a b) -> p a b", a=2), ALU.add).then_inc(mid_ready, 1)
                    mid_low(nm, slot)

                c0 = dve.snap(l * C_LAYER + C_MERGE)
                for c in range(5):
                    to_lo(c0, c + 2)
                merge(c0, (3, 4), 0, l * (NJ + NF) + 1)
                with dve.Fori(0, NJ - 2) as j:
                    c0 = dve.snap(l * C_LAYER + C_MERGE + j * 6)
                    for c in range(5, 11):
                        to_lo(c0, c + 2)
                    merge(c0, (9, 10), j + 1, l * (NJ + NF) + j + 2)

                c0 = dve.snap(l * C_LAYER + C_PLE)
                n2 = dve.snap(l * 2)
                for c in range(-7, -1):
                    if c == -2:
                        merge(c0, (-4, -3), NJ - 1, l * (NJ + NF) + NJ, slot=1)
                    to_lo(c0, c + 2)
                layer_norm_start(n2, c0)
                x_transposed(n2, 0, 0)
                normalised(n2, 1)
                x_low(n2 + 1, 0)
                x_transposed(n2, 0, 1)
                x_low(n2 + 1, 1)
                dve.wait_ge(lo_ready, c0 + 3 + RING)
                to_lo(c0, 3)
                second_tile(n2, l * 32 + 16)
                nc.vector.memset(hpad[:, :, 0:2], 0.0).then_inc(hpad_zeroed, 1)
                for j in range(NJ):
                    to_lo(c0, 4 + j)
                    dve.wait_ge(bank_read[j], l * USES[j] + (U_PLE[j] + 1 + 2))
                    v = ple[:, :, j * CH:(j + 1) * CH]
                    nc.vector.tensor_tensor(v, v, ple_sig.rearrange("p (t n) -> p t n", t=TT), ALU.mult)\
                      .then_inc(ple_ready, 1)

                def taps(half, turn, i):
                    dve.wait_ge(bank_read[half], turn + (l * (USES[half] - NF) + (U_MLP[half] + 2)))
                    for tap in (1, 0):
                        for b in range(2):
                            blk = half * (NB // 2) + b
                            ins = nc.vector.scalar_tensor_tensor(
                                out=conv[:, 2 * half + b, :], in0=hpad[:, 2 * half + b, tap:tap + SEQ],
                                scalar=feat[:, bass.ds(i * 2 + (PC_CW + tap * NB + blk), 1)],
                                in1=conv[:, 2 * half + b, :], op0=ALU.mult, op1=ALU.add)
                        if tap:
                            ins.then_inc(conv_first, 1)
                            dve.wait_ge(conv_first, 2 * turn + half + 1)
                    ins.then_inc(conv_ready, 1)

                def gated(turn, nm, slot=0):
                    dve.wait_ge(conv_ready, 2 * turn + 2)
                    dve.wait_ge(gelu_ready, turn + 1)
                    nc.vector.tensor_tensor(mid, conv[:, 0:2, :], conv[:, 2:4, :], ALU.mult).then_inc(mid_ready, 1)
                    mid_low(nm, slot)

                c0 = dve.snap(l * C_LAYER + C_MLP)
                to_lo(c0, 2)
                turn = dve.snap(l * NF)
                dve.wait_ge(hpad_zeroed, l + 1)
                taps(0, turn, 0)
                taps(1, turn, 0)
                with dve.Fori(0, NF - 1) as i:
                    c0 = dve.snap(l * C_LAYER + C_MLP + i * 3)
                    turn = dve.snap(l * NF + i)
                    nm = dve.snap(l * (NJ + NF) + NJ + i)
                    to_lo(c0, 3)
                    to_lo(c0, 4)
                    gated(turn, nm + 1)
                    next_turn = dve.snap(turn + 1)
                    taps(0, next_turn, i + 1)
                    to_lo(c0, 5)
                    taps(1, next_turn, i + 1)
                gated(l * NF + (NF - 1), l * (NJ + NF) + (NJ + NF), slot=1)
                c0 = dve.snap(l * C_LAYER + C_LAYER)
                layer_norm_start(n2 + 1, c0)
                with dve.If(DEPTH - 1 - l):
                    x_transposed(n2 + 1, 1, 0)
                normalised(n2 + 1, 1)
                with dve.If(DEPTH - 1 - l):
                    x_low(n2 + 2, 0)
                    x_transposed(n2 + 1, 1, 1)
                    x_low(n2 + 2, 1)
                second_tile(n2 + 1, l * 32 + 32)

        @block.gpsimd
        def _(pool):
            nc.gpsimd.memset(half_neg, -0.5).then_inc(exponent_set, 1)
            pool.wait_ge(exponent_set, 1)
            pool.wait_ge(x_in, 16)

            def to_lo(c0, c):
                s = c % RING
                pool.wait_ge(lo_ready, c0 + c + RING)
                pool.wait_ge(hi_ready, c0 + c + 1)
                nc.gpsimd.tensor_tensor(w_lo[:, s, :], raw[:, s, :], w_hi[:, s, :].bitcast(F32),
                                        ALU.subtract).then_inc(lo_ready, 1)

            def rstd(n, t):
                pool.wait_ge(ln_var_eps, n * TT + t + 1)
                nc.gpsimd.tensor_tensor(rs_ln[:, t:t + 1], ve_ln[:, t:t + 1], half_neg[:, 0:1], ALU.pow)\
                  .then_inc(ln_rstd, 1)

            def update_x(n, rows):
                pool.wait_ge(rows_in, rows)
                pool.wait_ge(ln_y, n * TT + 1)
                nc.gpsimd.tensor_tensor(X[:, 0, :], Y[:, 0, :], ln_gb[:, 0, :], ALU.mult).then_inc(x_by_g[0], 1)
                pool.wait_ge(x_by_g[0], n + 1)
                nc.gpsimd.tensor_tensor(X[:, 0, :], X[:, 0, :], ln_gb[:, 1, :], ALU.add).then_inc(x_updated[0], 1)

            with pool.Fori(0, DEPTH) as l:
                n2 = pool.snap(l * 2)
                for t in range(TT):
                    pool.wait_ge(x_updated[t], n2 + 1)
                nc.gpsimd.tensor_tensor(stat[:, 76:77], half_neg[:, 0:1], half_neg[:, 1:2], ALU.add)
                nc.gpsimd.tensor_scalar(X[:, :, :], X[:, :, :], ALPHA, 0.0, ALU.mult, ALU.add).then_inc(residual_ready, 1)
                with pool.Fori(0, NJ) as j:
                    pool.wait_ge(gn_var_eps, l * NJ + j + 1)
                    nc.gpsimd.tensor_tensor(rs_gn, ve_gn, half_neg, ALU.pow).then_inc(gn_rstd, 1)
                c0 = pool.snap(l * C_LAYER + C_PLE)
                to_lo(c0, 1)
                for t in range(TT):
                    rstd(n2, t)
                to_lo(c0, 2)
                update_x(n2, l * 32 + 16)
                for t in range(TT):
                    pool.wait_ge(x_updated[t], n2 + 2)
                nc.gpsimd.tensor_tensor(stat[:, 77:78], half_neg[:, 0:1], half_neg[:, 1:2], ALU.add)
                nc.gpsimd.tensor_scalar(X[:, :, :], X[:, :, :], ALPHA, 0.0, ALU.mult, ALU.add).then_inc(x_scaled, 1)
                pool.wait_ge(x_scaled, l + 1)
                pool.wait_ge(ple_ready, l * NJ + NJ)
                nc.gpsimd.tensor_tensor(X[:, :, :], X[:, :, :], ple, ALU.add).then_inc(residual_ready, 1)
                c0 = pool.snap(l * C_LAYER + C_LAYER)
                with pool.If(DEPTH - 1 - l):
                    to_lo(c0, 0)
                for t in range(TT):
                    rstd(n2 + 1, t)
                with pool.If(DEPTH - 1 - l):
                    to_lo(c0, 1)
                update_x(n2 + 1, l * 32 + 32)

        @block.tensor
        def _(pe):
            mm = nc.tensor.matmul

            def split_product(dst, st_hi, st_lo, mv_hi, mv_lo, start, stop):
                mm(dst, st_hi, mv_hi, start=start, stop=False)
                mm(dst, st_hi, mv_lo, start=False, stop=False)
                return mm(dst, st_lo, mv_hi, start=False, stop=stop)

            def weights_ready(c0, c):
                pe.wait_ge(lo_ready, c0 + c + 1 + RING)

            def transposed(c0, c, b, src_hi, src_lo, k0=0, start=True, stop=True):
                weights_ready(c0, c)
                s = c % RING
                for m in range(2):
                    for k in range(KT):
                        o = k * CH + m * P
                        ins = split_product(bank[b][:, m * SEQ:(m + 1) * SEQ], w_hi[:, s, o:o + P], w_lo[:, s, o:o + P],
                                            src_hi[:, k0 + k, :], src_lo[:, k0 + k, :],
                                            start and k == 0, stop and k == KT - 1 and (start or m == 1))
                ins.then_inc(chunk_done, 1)

            def by_token(c0, c, b, m=None):
                weights_ready(c0, c)
                s = c % RING
                for t in range(TT):
                    if m is not None:
                        pe.wait_ge(xT_lo_ready, m * 4 + 2 * t + 2)
                    for k in range(KT):
                        ins = split_product(bank[b][:, t * CH:(t + 1) * CH],
                                            xT_hi[:, k, t * P:(t + 1) * P], xT_lo[:, k, t * P:(t + 1) * P],
                                            w_hi[:, s, k * CH:(k + 1) * CH], w_lo[:, s, k * CH:(k + 1) * CH],
                                            k == 0, k == KT - 1)
                ins.then_inc(chunk_done, 1)

            def clear(dst):
                mm(dst, zero_r[:, 0:P], zero_r[:, :], start=True, stop=False)

            def keep_clock(n):
                for _ in range(n):
                    mm(bank[0][:, :], zero_r[:, 0:P], zero_r[:, :], start=True, stop=True)

            def from_mid(c0, c, n, slot=0, last=False):
                pe.wait_ge(mid_lo_ready, n)
                weights_ready(c0, c)
                s = c % RING
                for t in range(TT):
                    for h in range(2):
                        for k in range(2):
                            o = k * D + h * 512
                            ins = split_product(acc[2 * t + h][:, :],
                                                mid_hi[:, slot, k, t * P:(t + 1) * P],
                                                mid_lo[:, slot, k, t * P:(t + 1) * P],
                                                w_hi[:, s, o:o + 512], w_lo[:, s, o:o + 512], False, last and k == 1)
                        if last and 2 * t + h < 3:
                            ins.then_inc(acc_part_done, 1)
                ins.then_inc(chunk_done, 1)

            def transpose_y(n, t):
                pe.wait_ge(ln_y, n * TT + t + 1)
                for k in range(KT):
                    ins = nc.tensor.transpose(acc[2 * t + k // 4][:, (k % 4) * P:(k % 4 + 1) * P],
                                              Y[:, t, k * P:(k + 1) * P], ident)
                    if k % 4 == 3:
                        ins.then_inc(lnT_done, 1)

            pe.wait_ge(zeros_set, 1)
            pe.wait_ge(xT_hi_ready, 1)
            pe.wait_ge(bank_read[0], 1)
            keep_clock(10)
            with pe.Fori(0, DEPTH) as l:
                with pe.Fori(0, NJ) as j:
                    it = pe.snap(l * NJ + j)
                    it2 = pe.snap(it * 2)
                    c0 = pe.snap(l * C_LAYER + j * C_MIX)
                    used = [pe.snap(l * USES[b] + j * 5) for b in range(3)]

                    def scores(a):
                        for g in range(NG):
                            mm(acc[0][:, g * P:(g + 1) * P], qk[:, 2 * g, a, 0:P], qk[:, 2 * g + 1, a, 0:P],
                               start=True, stop=True)
                        for g in range(NG):
                            ins = mm(acc[1 + g // 2][:, (g % 2) * SEQ:(g % 2 + 1) * SEQ],
                                     qk[:, 2 * g, a, P:SEQ], qk[:, 2 * g + 1, a, :], start=True, stop=True)
                        ins.then_inc(scores_done, 1)

                    def transpose_prob(a):
                        pe.wait_ge(prob_ready, it2 + a + 1)
                        for g in range(NG):
                            for o, src in enumerate((g * P, 384 + g * 256, 384 + g * 256 + P)):
                                ins = nc.tensor.transpose(acc[g][:, o * P:(o + 1) * P], prob[:, src:src + P], ident)
                        ins.then_inc(probT_done, 1)

                    def attend(a):
                        for g in range(NG):
                            mm(acc[a][:, 0:SEQ], att_v[:, g, 0, a * P:(a + 1) * P], probT[:, a, g, 0:SEQ],
                               start=(g == 0), stop=False)
                            ins = mm(acc[a][:, P:SEQ], att_v[:, g, 1, a * P:(a + 1) * P], probT[:, a, g, SEQ:384],
                                     start=False, stop=(g == NG - 1))
                        ins.then_inc(pv_done, 1)

                    for c in range(C_MIX):
                        b = c % 3
                        pe.wait_ge(bank_read[b], used[b] + (c // 3 + 1))
                        if c in (0, 9, 10, 11, 12):
                            by_token(c0, c, b, l * 2 if c == 0 else None)
                        else:
                            transposed(c0, c, b, xT_hi, xT_lo)
                        if c == 7:
                            pe.wait_ge(bank_read[0], used[0] + 4)
                            pe.wait_ge(attn_lo_ready, it2 + 2)
                            pe.wait_ge(ret_affine, it + 1)
                            scores(0)
                        if c == 10:
                            pe.wait_ge(angle_in, 32)
                            pe.wait_ge(roped_ready, it2 + 2)
                            for h in range(2):
                                mm(acc[3][:, 0:SEQ], roped[:, 1, h, 0:P], roped[:, 0, h, :], start=(h == 0), stop=(h == 1))
                            for h in range(2):
                                ins = mm(acc[3][:, SEQ:384], roped[:, 1, h, P:SEQ], roped[:, 0, h, P:SEQ],
                                         start=(h == 0), stop=(h == 1))
                            ins.then_inc(ret_scores_done, 1)
                            transpose_prob(0)
                        if c == 11:
                            pe.wait_ge(probT_copied, it2 + 1)
                            scores(1)
                        if c == 12:
                            pe.wait_ge(decayed_lo_ready, it + 1)
                            pe.wait_ge(bank_read[0], used[0] + 5)
                            pe.wait_ge(bank_read[3], l * USES[3] + j + 1)
                            for o, (dst, t) in enumerate(((bank[3], 0), (acc[3], 0), (acc[3], 1))):
                                v = slice(o * P, (o + 1) * P)
                                ins = split_product(dst[:, :], decayed_hi[:, v], decayed_lo[:, v],
                                                    rv_hi[:, t, :], rv_lo[:, t, :], o < 2, o != 1)
                            ins.then_inc(ret_av_done, 1)
                        if c == 13:
                            transpose_prob(1)
                    pe.wait_ge(probT_copied, it2 + 2)
                    pe.wait_ge(bank_read[0], used[0] + 6)
                    attend(0)
                    attend(1)
                    pe.wait_ge(ret_y_ready, it + 1)
                    for t in range(TT):
                        for k in range(4):
                            ins = nc.tensor.transpose(acc[2 + k // 2][:, (k % 2) * SEQ + t * P:(k % 2) * SEQ + (t + 1) * P],
                                                      ret_y[:, t, k * P:(k + 1) * P], ident)
                    ins.then_inc(ret_yT_done, 1)

                def gate(c0, c, b, j):
                    pe.wait_ge(bank_read[b], l * USES[b] + j + (U_MERGE[b] + 1))
                    transposed(c0, c, b, xT_hi, xT_lo)

                def mixers(c0, c, j):
                    pe.wait_ge(bank_read[2], l * USES[2] + j + (U_MERGE[2] + 1))
                    clear(bank[2][:, :])
                    transposed(c0, c, 2, ret_hi, ret_lo, 0, start=False, stop=False)
                    transposed(c0, c + 1, 2, ret_hi, ret_lo, KT, start=False)
                    pe.wait_ge(bank_read[3], l * USES[3] + j + (U_MERGE[3] + 1))
                    transposed(c0, c + 2, 3, attn_hi, attn_lo)

                c0 = pe.snap(l * C_LAYER + C_MERGE)
                gate(c0, 0, 0, 0)
                gate(c0, 1, 1, 0)
                pe.wait_ge(ret_lo_ready, l * NJ + NJ)
                pe.wait_ge(attn_lo_ready, l * (2 * NJ) + 2 * NJ + 2)
                pe.wait_ge(ret_affine, l * NJ + NJ + 1)
                pe.wait_ge(zeros_set, 1)
                for a in range(4):
                    clear(acc[a][:, :])
                mixers(c0, 2, 0)
                with pe.Fori(0, NJ - 2) as j:
                    c0 = pe.snap(l * C_LAYER + C_MERGE + j * 6)
                    gate(c0, 5, 0, j + 1)
                    from_mid(c0, 6, l * (NJ + NF) + j + 1)
                    gate(c0, 7, 1, j + 1)
                    mixers(c0, 8, j + 1)
                c0 = pe.snap(l * C_LAYER + C_PLE)
                gate(c0, -7, 0, NJ - 1)
                gate(c0, -6, 1, NJ - 1)
                mixers(c0, -5, NJ - 1)
                from_mid(c0, -2, l * (NJ + NF) + NJ - 1)
                from_mid(c0, -1, l * (NJ + NF) + NJ, slot=1, last=True)

                for u in range(2):
                    weights_ready(c0, u)
                    for t in range(TT):
                        b = 2 * u + t
                        pe.wait_ge(bank_read[b], l * USES[b] + (U_PLE[b] + 1))
                        for k in range(2):
                            o = 1024 + k * SEQ + t * P
                            ins = split_product(bank[b][:, :], w_hi[:, u, o:o + P], w_lo[:, u, o:o + P],
                                                w_hi[:, u, k * 512:(k + 1) * 512], w_lo[:, u, k * 512:(k + 1) * 512],
                                                k == 0, k == 1)
                        if u == 1 and t == 0:
                            transpose_y(l * 2, 0)
                    ins.then_inc(chunk_done, 1)
                pe.wait_ge(bank_read[0], l * USES[0] + (U_PLE[0] + 2))
                keep_clock(2)
                transpose_y(l * 2, 1)
                keep_clock(8)
                for j in range(NJ):
                    pe.wait_ge(bank_read[j], l * USES[j] + (U_PLE[j] + 2))
                    by_token(c0, 2 + j, j, l * 2 + 1 if j == 0 else None)

                def up(c0, c, half, i):
                    pe.wait_ge(bank_read[half], l * USES[half] + i + (U_MLP[half] + 1))
                    transposed(c0, c, half, xT_hi, xT_lo)

                c0 = pe.snap(l * C_LAYER + C_MLP)
                for a in range(4):
                    clear(acc[a][:, :])
                up(c0, 0, 0, 0)
                up(c0, 1, 1, 0)
                with pe.Fori(0, NF - 1) as i:
                    c0 = pe.snap(l * C_LAYER + C_MLP + i * 3)
                    up(c0, 2, 0, i + 1)
                    up(c0, 3, 1, i + 1)
                    from_mid(c0, 4, l * (NJ + NF) + i + (NJ + 1))
                c0 = pe.snap(l * C_LAYER + C_LAYER)
                from_mid(c0, -1, l * (NJ + NF) + (NJ + NF), slot=1, last=True)
                with pe.If(DEPTH - 1 - l):
                    pe.wait_ge(bank_read[0], l * USES[0] + (USES[0] + 1))
                    keep_clock(7)
                    transpose_y(l * 2 + 1, 0)
                    keep_clock(14)
                    transpose_y(l * 2 + 1, 1)


def constant_table():
    t = np.zeros((P, NCC), np.float64)
    q = np.arange(P)[:, None]
    k = np.arange(2 * P)[None, :]
    dist = q + P - k
    for g, (window, dilation) in enumerate(GROUPS):
        ok = (dist >= 0) & (dist <= window) & (dist % dilation == 0)
        t[:, CC_MASK + g * 256:CC_MASK + (g + 1) * 256] = np.where(ok, 0.0, MASKED)
    rel = k - q
    for h in range(RH):
        log_gamma = np.log1p(-2.0 ** (-5.0 - h))
        t[:, CC_DEC + h * 256:CC_DEC + (h + 1) * 256] = np.where(
            rel >= 0, np.exp(log_gamma * np.maximum(rel, 0)), 0.0) * RET_SCALE
    t[:, CC_ID:CC_ID + P] = np.eye(P)
    t = t.astype(np.float32)
    t[:, CC_FREQ] = np.power(np.float32(10000.0), -np.arange(P, dtype=np.float32) / np.float32(P))
    return t


def kernel(**inputs):
    import concourse.bacc as _bacc
    from concourse.bass_utils import run_bass_kernel_spmd as _run

    a = {n: np.ascontiguousarray(v) for n, v in inputs.items()}

    def by_feature(v):
        return v.reshape(DEPTH, -1, P).transpose(0, 2, 1)

    feature_params = np.concatenate(
        [by_feature(a["conv_w"][:, i]) for i in range(3)] +
        [by_feature(a[n]) for n in ("conv_b", "ret_gn_g", "ret_gn_b", "ln1_g", "ln1_b", "ln2_g", "ln2_b")], axis=2)
    wp = a["w_ple_proj"].reshape(DEPTH, 2, P, 2, 512).transpose(0, 3, 2, 1, 4).reshape(DEPTH, 2, P, 1024)
    pt = a["p"].reshape(DEPTH, SEQ, 2, P).transpose(0, 3, 2, 1).reshape(DEPTH, 1, P, 2 * SEQ)
    arrays = {
        "x": a["x"].reshape(SEQ, D), "xT": a["x"].reshape(SEQ, D).T, "positions": a["positions"],
        "w_in": a["w_in"], "w_attn_proj": a["w_attn_proj"], "w_ret_proj": a["w_ret_proj"], "w_out": a["w_out"],
        "w_up": a["w_up"], "w_down": a["w_down"], "w_ple_gate": a["w_ple_gate"],
        "ple_operands": np.concatenate([wp, np.repeat(pt, 2, axis=1)], axis=3),
        "ln_rows": np.concatenate([a["ln1_g"], a["ln1_b"], a["ln2_g"], a["ln2_b"]], axis=1),
        "feature_params": feature_params, "constants": constant_table(),
    }
    arrays = {n: np.ascontiguousarray(v) for n, v in arrays.items()}
    nc = _bacc.Bacc("TRN2", target_bir_lowering=False, num_devices=1, dynamic_dma_scratch_size=1024)
    aps = [nc.dram_tensor(n, v.shape, mybir.dt.from_np(v.dtype), kind="ExternalInput").ap() for n, v in arrays.items()]
    out = nc.dram_tensor("out", (SEQ, D), F32, kind="ExternalOutput").ap()
    program(nc, *aps, out)
    r = _run(nc, [arrays], core_ids=[0])
    return r.results[0]["out"].reshape(1, SEQ, D)
```
